# Optimizing a Trainium2 kernel written in Bass

```python
import math
import jax, jax.numpy as jnp
from jax import lax
import numpy as np

D_MODEL = 1024
BATCH = 1
SEQ = 256
DEPTH = 1

POOL_WINDOWS = (2, 4, 8, 16)
POOL_WIDTH = D_MODEL // 2
POOL_GROUP = POOL_WIDTH // len(POOL_WINDOWS)
HEAD_DIM = 64
ATTN_GROUPS = ((128, 1), (512, 4), (2048, 16))
HEADS_PER_GROUP = 4
N_HEADS = HEADS_PER_GROUP * len(ATTN_GROUPS)
ATTN_WIDTH = N_HEADS * HEAD_DIM
ATTN_OUT_WIDTH = HEADS_PER_GROUP * HEAD_DIM
ATTN_BLOCK = 128
ROT_DIM = HEAD_DIM // 4
ROPE_THETA = 500000.0
N_BRANCHES = 2
IN_WIDTH = POOL_WIDTH + 3 * ATTN_WIDTH + N_BRANCHES * D_MODEL
N_EXPERTS = 32
TOP_K = 4
D_EXPERT = D_MODEL
SWIGLU_ALPHA = 1.702
SWIGLU_LIMIT = 7.0
MOE_BLOCK = 256
DN_ALPHA = (2.0 * DEPTH) ** 0.25
DN_BETA = (8.0 * DEPTH) ** -0.25
LN_EPS = 1e-5
NEG_INF = -1e30

kernel_name = "hybrid_pool_dilated_attn_moe_deepnorm_adaln"

def layer_norm(x, g=None, b=None):
    xf = x.astype(jnp.float32)
    mu = jnp.mean(xf, axis=-1, keepdims=True)
    var = jnp.mean(jnp.square(xf - mu), axis=-1, keepdims=True)
    y = (xf - mu) * lax.rsqrt(var + LN_EPS)
    if g is not None:
        y = y * g.astype(jnp.float32) + b.astype(jnp.float32)
    return y.astype(x.dtype)

def pool_mixer(xp, pool_w, pool_scale):
    B, S, _ = xp.shape
    G = len(POOL_WINDOWS)
    xf = xp.reshape(B, S, G, POOL_GROUP).astype(jnp.float32)
    cs = jnp.cumsum(xf, axis=1)
    cs0 = jnp.concatenate([jnp.zeros_like(cs[:, :1]), cs], axis=1)
    t = jnp.arange(S)
    means = []
    for g, w in enumerate(POOL_WINDOWS):
        c_g = cs0[:, :, g]
        lo = jnp.concatenate([jnp.zeros((B, w - 1, POOL_GROUP), jnp.float32),
                              c_g[:, :S - w + 1]], axis=1)
        cnt = jnp.minimum(t + 1, w).astype(jnp.float32)[None, :, None]
        means.append((c_g[:, 1:] - lo) / cnt)
    mixed = (jnp.stack(means, axis=2) - xf).astype(xp.dtype)
    y = jnp.einsum('bsgc,gcd->bsgd', mixed, pool_w).reshape(B, S, POOL_WIDTH)
    return y * pool_scale

def partial_rotary(x, positions):
    half = ROT_DIM // 2
    inv_freq = jnp.power(ROPE_THETA, -jnp.arange(half, dtype=jnp.float32) * (2.0 / ROT_DIM))
    ang = positions.astype(jnp.float32)[..., None] * inv_freq
    cos = jnp.cos(ang)[:, :, None, :]
    sin = jnp.sin(ang)[:, :, None, :]
    xf = x.astype(jnp.float32)
    x1, x2 = xf[..., :half], xf[..., half:ROT_DIM]
    out = jnp.concatenate([x1 * cos - x2 * sin, x2 * cos + x1 * sin, xf[..., ROT_DIM:]], axis=-1)
    return out.astype(x.dtype)

def dilated_window_attention(q, k, v, window, dilation):
    B, S, H, E = q.shape
    n_back = window // dilation
    L = S // dilation
    nb = -(-L // ATTN_BLOCK)
    Lp = nb * ATTN_BLOCK

    def to_blocks(a):
        a = a.reshape(B, L, dilation, H, E).transpose(0, 2, 1, 3, 4)
        a = jnp.pad(a, ((0, 0), (0, 0), (0, Lp - L), (0, 0), (0, 0)))
        return a.reshape(B, dilation, nb, ATTN_BLOCK, H, E)

    def with_prev(a):
        prev = jnp.pad(a[:, :, :-1], ((0, 0), (0, 0), (1, 0), (0, 0), (0, 0), (0, 0)))
        return jnp.concatenate([prev, a], axis=3)

    qb = to_blocks(q)
    kk = with_prev(to_blocks(k))
    vv = with_prev(to_blocks(v))
    s = jnp.einsum('bdnqhe,bdnkhe->bdnhqk', qb, kk,
                   preferred_element_type=jnp.float32) * (E ** -0.5)
    qi = jnp.arange(ATTN_BLOCK)[:, None]
    kj = jnp.arange(2 * ATTN_BLOCK)[None, :]
    dist = ATTN_BLOCK + qi - kj
    band = (dist >= 0) & (dist <= n_back)
    has_prev = (jnp.arange(nb)[:, None, None] > 0) | (kj[None] >= ATTN_BLOCK)
    mask = band[None] & has_prev
    s = jnp.where(mask[None, None, :, None], s, NEG_INF)
    m = jnp.max(s, axis=-1, keepdims=True)
    p = jnp.exp(s - m)
    den = jnp.sum(p, axis=-1, keepdims=True)
    o = jnp.einsum('bdnhqk,bdnkhe->bdnqhe', p.astype(v.dtype), vv,
                   preferred_element_type=jnp.float32)
    o = o / jnp.swapaxes(den, 3, 4)
    lse = jnp.swapaxes((m + jnp.log(den))[..., 0], 3, 4)
    o = o.reshape(B, dilation, Lp, H, E)[:, :, :L].transpose(0, 2, 1, 3, 4).reshape(B, S, H, E)
    lse = lse.reshape(B, dilation, Lp, H)[:, :, :L].transpose(0, 2, 1, 3).reshape(B, S, H)
    return o, lse

def clamped_swiglu_expert(xb, wg, bg, wu, bu, wd, bd):
    g = xb @ wg + bg
    up = xb @ wu + bu
    g = jnp.minimum(g, SWIGLU_LIMIT)
    up = jnp.clip(up, -SWIGLU_LIMIT, SWIGLU_LIMIT)
    h = g * jax.nn.sigmoid(SWIGLU_ALPHA * g) * (up + 1.0)
    return h @ wd + bd

def moe_ffn(u, w_router, b_router, w_gate, b_gate, w_up, b_up, w_down, b_down):
    B, S, D = u.shape
    N = B * S
    A = N * TOP_K
    xt = u.reshape(N, D)
    logits = (xt @ w_router).astype(jnp.float32) + b_router.astype(jnp.float32)
    top_val, top_idx = lax.top_k(logits, TOP_K)
    probs = jax.nn.softmax(top_val, axis=-1)
    eid = top_idx.reshape(A).astype(jnp.int32)
    tid = jnp.arange(A, dtype=jnp.int32) // TOP_K
    wgt = probs.reshape(A)
    order = jnp.argsort(eid)
    se = eid[order]
    counts = jax.ops.segment_sum(jnp.ones((A,), jnp.int32), eid, num_segments=N_EXPERTS)
    offsets = jnp.cumsum(counts) - counts
    padded = (counts + MOE_BLOCK - 1) // MOE_BLOCK * MOE_BLOCK
    pad_ends = jnp.cumsum(padded)
    pad_offsets = pad_ends - padded
    dest = pad_offsets[se] + jnp.arange(A, dtype=jnp.int32) - offsets[se]
    nblk = -(-A // MOE_BLOCK) + N_EXPERTS
    P = nblk * MOE_BLOCK
    row_tok = jnp.full((P,), N, jnp.int32).at[dest].set(tid[order])
    row_w = jnp.zeros((P,), jnp.float32).at[dest].set(wgt[order])
    blk_exp = jnp.minimum(jnp.searchsorted(pad_ends, jnp.arange(nblk) * MOE_BLOCK, side='right'),
                          N_EXPERTS - 1).astype(jnp.int32)
    xpad = jnp.concatenate([xt, jnp.zeros((1, D), xt.dtype)], axis=0)
    xs = xpad[row_tok].reshape(nblk, MOE_BLOCK, D)

    def expert_block(args):
        xb, e = args
        return clamped_swiglu_expert(xb, w_gate[e], b_gate[e], w_up[e], b_up[e], w_down[e], b_down[e])

    ys = lax.map(expert_block, (xs, blk_exp)).reshape(P, D)
    out = jax.ops.segment_sum(ys.astype(jnp.float32) * row_w[:, None], row_tok,
                              num_segments=N + 1)[:N]
    return out.astype(u.dtype).reshape(B, S, D)

def setup_inputs(seed: int = 0) -> dict:
    key = jax.random.key(seed)
    ks = jax.random.split(key, 26)
    nrm = lambda k, shape, s: jax.random.normal(k, shape, jnp.float32) * s
    Dd, L = D_MODEL, DEPTH
    G = len(POOL_WINDOWS)
    x = jax.random.normal(ks[0], (BATCH, SEQ, Dd), jnp.float32)
    c = jax.random.normal(ks[1], (BATCH, Dd), jnp.float32)
    offs = jax.random.randint(ks[2], (BATCH, 1), 0, 4096, jnp.int32)
    positions = (jnp.arange(SEQ, dtype=jnp.int32)[None, :] + offs).astype(jnp.int32)
    return {
        "x": x,
        "c": c,
        "positions": positions,
        "w_ada": nrm(ks[3], (L, Dd, 6 * Dd), 0.1 * Dd ** -0.5),
        "b_ada": nrm(ks[4], (L, 6 * Dd), 0.01),
        "w_in": nrm(ks[5], (L, Dd, IN_WIDTH), Dd ** -0.5),
        "pool_w": nrm(ks[6], (L, G, POOL_GROUP, POOL_GROUP), POOL_GROUP ** -0.5),
        "pool_scale": 1.0 + nrm(ks[7], (L, POOL_WIDTH), 0.1),
        "w_pool_out": nrm(ks[8], (L, POOL_WIDTH, Dd), POOL_WIDTH ** -0.5),
        "w_attn_out": nrm(ks[9], (L, ATTN_OUT_WIDTH, Dd), ATTN_OUT_WIDTH ** -0.5),
        "w_o": nrm(ks[10], (L, Dd, Dd), DN_BETA * Dd ** -0.5),
        "ln1_g": 1.0 + nrm(ks[11], (L, Dd), 0.02),
        "ln1_b": nrm(ks[12], (L, Dd), 0.02),
        "w_router": nrm(ks[13], (L, Dd, N_EXPERTS), Dd ** -0.5),
        "b_router": nrm(ks[14], (L, N_EXPERTS), 0.01),
        "w_gate": nrm(ks[15], (L, N_EXPERTS, Dd, D_EXPERT), Dd ** -0.5),
        "b_gate": nrm(ks[16], (L, N_EXPERTS, D_EXPERT), 0.01),
        "w_up": nrm(ks[17], (L, N_EXPERTS, Dd, D_EXPERT), Dd ** -0.5),
        "b_up": nrm(ks[18], (L, N_EXPERTS, D_EXPERT), 0.01),
        "w_down": nrm(ks[19], (L, N_EXPERTS, D_EXPERT, Dd), DN_BETA * D_EXPERT ** -0.5),
        "b_down": nrm(ks[20], (L, N_EXPERTS, Dd), 0.01),
        "ln2_g": 1.0 + nrm(ks[21], (L, Dd), 0.02),
        "ln2_b": nrm(ks[22], (L, Dd), 0.02),
    }

def reference(x, c, positions, w_ada, b_ada, w_in, pool_w, pool_scale, w_pool_out, w_attn_out,
              w_o, ln1_g, ln1_b, w_router, b_router, w_gate, b_gate, w_up, b_up, w_down, b_down,
              ln2_g, ln2_b):
    B, S, D = x.shape
    splits = [POOL_WIDTH, POOL_WIDTH + ATTN_WIDTH, POOL_WIDTH + 2 * ATTN_WIDTH,
              POOL_WIDTH + 3 * ATTN_WIDTH, POOL_WIDTH + 3 * ATTN_WIDTH + D_MODEL]
    for l in range(DEPTH):
        ada = jax.nn.silu(c) @ w_ada[l] + b_ada[l]
        shift1, scale1, gate1, shift2, scale2, gate2 = jnp.split(ada[:, None, :], 6, axis=-1)

        u = layer_norm(x) * (1.0 + scale1) + shift1
        proj = u @ w_in[l]
        xp, q, k, v, g_p, g_a = jnp.split(proj, splits, axis=-1)

        pool_y = pool_mixer(xp, pool_w[l], pool_scale[l])

        q = partial_rotary(q.reshape(B, S, N_HEADS, HEAD_DIM), positions)
        k = partial_rotary(k.reshape(B, S, N_HEADS, HEAD_DIM), positions)
        v = v.reshape(B, S, N_HEADS, HEAD_DIM)
        outs, lses = [], []
        for gi, (window, dilation) in enumerate(ATTN_GROUPS):
            hs = slice(gi * HEADS_PER_GROUP, (gi + 1) * HEADS_PER_GROUP)
            o, lse = dilated_window_attention(q[:, :, hs], k[:, :, hs], v[:, :, hs], window, dilation)
            outs.append(o)
            lses.append(lse)
        mix_w = jax.nn.softmax(jnp.stack(lses, axis=0), axis=0)
        attn = jnp.sum(mix_w[..., None] * jnp.stack(outs, axis=0), axis=0)
        attn = attn.reshape(B, S, ATTN_OUT_WIDTH).astype(x.dtype)

        merged = (jax.nn.sigmoid(g_p) * (pool_y @ w_pool_out[l])
                  + jax.nn.sigmoid(g_a) * (attn @ w_attn_out[l]))
        mix = merged @ w_o[l]
        x = layer_norm(DN_ALPHA * x + (1.0 + gate1) * mix, ln1_g[l], ln1_b[l])

        u2 = layer_norm(x) * (1.0 + scale2) + shift2
        ffn = moe_ffn(u2, w_router[l], b_router[l], w_gate[l], b_gate[l], w_up[l], b_up[l],
                      w_down[l], b_down[l])
        x = layer_norm(DN_ALPHA * x + (1.0 + gate2) * ffn, ln2_g[l], ln2_b[l])
    return x


_drawn_inputs = setup_inputs


def setup_inputs(seed=0):
    import zlib

    import numpy as np

    out = dict(_drawn_inputs(seed))
    spreads = {}
    factors = {'b_router': 3.385,
     'b_gate': 22.614,
     'b_up': 33.017,
     'b_down': 8.0,
     'ln2_g': 7.593,
     'ln2_b': 7.795}
    for name, (base, spread) in spreads.items():
        noise = np.random.default_rng([zlib.crc32(name.encode()), seed]).standard_normal(out[name].shape)
        drawn = base * np.exp(spread * noise) if base else spread * noise
        out[name] = __import__('jax').numpy.asarray(drawn.astype(out[name].dtype))
    for name, factor in factors.items():
        out[name] = (out[name] * factor).astype(out[name].dtype)
    return out
```

```python
import math
from contextlib import ExitStack

import numpy as np

import concourse.bass as bass
from concourse import mybir

F32 = mybir.dt.float32
BF16 = mybir.dt.bfloat16
I32 = mybir.dt.int32
U32 = mybir.dt.uint32
ALU = mybir.AluOpType
ACT = mybir.ActivationFunctionType
AX = mybir.AxisListType

P = 128
D = 1024
S = 256
NT = S // P
KT = D // P
HALF = 512
POOL_WIDTH = D // 2
POOL_WINDOWS = (2, 4, 8, 16)
PG = len(POOL_WINDOWS)
HEAD_DIM = 64
GROUPS = ((128, 1), (512, 4), (2048, 16))
NG = len(GROUPS)
HEAD_SLOTS = 4
ATTN_WIDTH = NG * HEAD_SLOTS * HEAD_DIM
QT = ATTN_WIDTH // P
ROT_DIM = HEAD_DIM // 4
ROPE_THETA = 500000.0
NE = 32
TOP_K = 4
CAP = 64
CHUNKS = S // CAP - 1
SWIGLU_ALPHA = 1.702
SWIGLU_LIMIT = 7.0
DN_ALPHA = 2.0 ** 0.25
LN_EPS = 1e-5
NEG_INF = -1e30

SLOT = 4096
SLOTS = 8
FRONT_SLOTS = 6
UNITS = 6
BODY = 4
TURNS = NE // BODY

FRONT = [("ada", 0), ("ada", 1), ("ada", 2), ("ada", 3), ("in", 1), ("in", 2), ("in", 3), ("ada", 4),
         ("in", 4), ("ada", 5), ("in", 5), ("ada", 6), ("in", 0), ("ada", 7), ("in", 6), ("ada", 8),
         ("in", 7), ("ada", 9), ("in", 8), ("ada", 10), ("in", 9), ("ada", 11), ("attn_out", 0),
         ("pool_out", 0), ("o", 0), ("o", 1)]
IN_COLS = [(0, 512), (512, 1024), (1024, 1536), (1536, 2048), (2048, 2560), (2560, 2816)] + \
          [(2816 + 512 * j, 3328 + 512 * j) for j in range(4)]
SLOT_OF = {u: n % FRONT_SLOTS for n, u in enumerate(FRONT)}
TURN_OF = {u: n // FRONT_SLOTS + 1 for n, u in enumerate(FRONT)}
FILLS = [sum(n % FRONT_SLOTS == s for n in range(len(FRONT))) if s < FRONT_SLOTS else 0 for s in range(SLOTS)]
RING = [6, 7, 2, 3, 4, 5, 0, 1]

C_IDENT, C_PERM, C_TRI = 0, 128, 256
C_RANKS, C_EXPERTS, C_PICK, C_RCNT = 384, 448, 480, 512
C_FREQ, C_EPS, C_DROP1, C_DROP2, C_ONE = 576, 577, 578, 579, 580
N_CONST = 581
PADDED = NE + 2

TWO_PI_PARTS = []
_rest = 2.0 * math.pi
for _bits in (8, 8, 8, 24):
    _m, _e = math.frexp(_rest)
    TWO_PI_PARTS.append(math.ldexp(round(_m * 2 ** _bits), _e - _bits))
    _rest -= TWO_PI_PARTS[-1]
ROUND = 1.5 * 2.0 ** 23


def constants():
    c = np.zeros((P, N_CONST), np.float32)
    p = np.arange(P)
    c[:, C_IDENT:C_IDENT + P] = np.eye(P)
    for m in range(P):
        j = m % HEAD_DIM
        if j < ROT_DIM // 2:
            c[m + ROT_DIM // 2, C_PERM + m] = -1.0
        elif j < ROT_DIM:
            c[m - ROT_DIM // 2, C_PERM + m] = 1.0
    c[:, C_TRI:C_TRI + P] = p[:, None] < p[None, :]
    c[:, C_RANKS:C_RANKS + CAP] = np.arange(1, CAP + 1)
    c[:, C_EXPERTS:C_EXPERTS + NE] = np.arange(NE)
    c[:, C_PICK:C_PICK + NE] = (p % 32)[:, None] == np.arange(NE)[None]
    t = np.arange(16)
    for g, w in enumerate(POOL_WINDOWS):
        c[:, C_RCNT + 16 * g:C_RCNT + 16 * g + 16] = 1.0 / np.minimum(t + 1, w)
    j = p % HEAD_DIM
    freq = np.power(ROPE_THETA, -(j % (ROT_DIM // 2)) * (2.0 / ROT_DIM))
    c[:, C_FREQ] = np.where(j < ROT_DIM, freq, 0.0)
    c[:, C_EPS] = LN_EPS
    c[:, C_DROP1] = -(p >= 32).astype(np.float32)
    c[:, C_DROP2] = -(p >= 64).astype(np.float32)
    c[:, C_ONE] = 1.0
    q, k = np.arange(P)[:, None], np.arange(P)[None]
    masks = np.zeros((P, NG, 2, P), np.float32)
    for g, (window, dilation) in enumerate(GROUPS):
        for tile, dist in enumerate((P + q - k, q - k)):
            ok = (dist >= 0) & (dist <= window) & (dist % dilation == 0)
            masks[:, g, tile] = np.where(ok, 0.0, NEG_INF)
    return c, masks.reshape(P, NG * 2 * P)


def layer_kernel(nc, x, c, positions, w_ada, b_ada, w_in, pool_w, pool_scale, w_pool_out, w_attn_out, w_o,
                 ln1_g, ln1_b, w_router, b_router, w_gate, b_gate, w_up, b_up, w_down, b_down, ln2_g, ln2_b,
                 const_table, mask_table, out):
    ctx = ExitStack()
    with ctx:
        def sb(name, shape, dt=F32):
            return ctx.enter_context(nc.sbuf_tensor(name, shape, dt))

        def sem(name):
            return ctx.enter_context(nc.semaphore(name))

        ring = sb("ring", [P, SLOTS * SLOT])
        const = sb("const", [P, N_CONST])
        x_tok = sb("x_tok", [P, NT, D])
        ln_tok = sb("ln_tok", [P, NT * D])
        feat_region = sb("feat_region", [P, KT * S])
        pool_region = sb("pool_region", [P, 2048])
        gate_region = sb("gate_region", [P, 4096])
        attn_region = sb("attn_region", [P, 704])
        acc_region = sb("acc_region", [P, 1024])
        row_region = sb("row_region", [P, 4096])
        bias_parts = sb("bias_parts", [96, 2, D], BF16)
        ada_parts = sb("ada_parts", [96, HALF], BF16)
        router_w = sb("router_w", [P, KT + 1, NE])
        small = sb("small", [P, 104])

        def view(t, start, size, dt=F32, parts=P):
            a = t[0:parts, start:start + size]
            return a if dt is F32 else a.bitcast(dt)

        late = FRONT_SLOTS * SLOT
        qk = view(ring, late, 2 * QT * S).rearrange("p (j t) -> p j t", j=2 * QT)
        v_tok = view(ring, late + 3072, NT * ATTN_WIDTH).rearrange("p (t n) -> p t n", t=NT)
        probs = view(ring, late + 4608, 1152)
        probs_t = view(ring, late + 5760, 1152).rearrange("p (g n) -> p g n", g=NG)
        cos = view(ring, late + 6912, S)
        sin = view(ring, late + 7168, S)
        masks = view(ring, late + 7424, NG * 2 * P).rearrange("p (g k n) -> p g k n", g=NG, k=2)
        rot_tmp = view(ring, late + 4608, 2 * S).rearrange("p (j t) -> p j t", j=2)
        pos_i = view(ring, late + 5760, S, I32)
        angle = view(ring, late + 5760 + S, S)
        turns = view(ring, late + 5760 + 2 * S, S)

        xn = ln_tok[:, :].rearrange("p (t n) -> p t n", t=NT)
        u2 = xn
        u_t = feat_region[:, :].rearrange("p (k t) -> p k t", k=KT)
        xp_t = view(pool_region, 0, PG * S).rearrange("p (g t) -> p g t", g=PG)
        mixed = view(pool_region, 1024, PG * S).rearrange("p (g t) -> p g t", g=PG)
        ln_rows = pool_region[:, :].rearrange("p (r n) -> p r n", r=2)
        b_down_sb = view(gate_region, 3072, D, parts=NE)
        gates = gate_region[:, :].rearrange("p (j t) -> p j t", j=2 * KT)
        pool_tmp = gates[:, 12:16, :]
        bias_raw = view(gate_region, 0, 2 * D, parts=96).rearrange("p (m n) -> p m n", m=2)
        attn_t = view(attn_region, 0, 2 * S).rearrange("p (j t) -> p j t", j=2)
        ada_acc = acc_region[:, :].rearrange("p (b n) -> p b n", b=2)
        ada_rows = row_region[:, :].rearrange("p (r n) -> p r n", r=4)
        pool_w_sb = view(row_region, 3584, PG * P).rearrange("p (g d) -> p g d", g=PG)
        b_ada_raw = view(feat_region, 0, HALF, parts=96)

        c_col, c_silu, c_sig = small[:, 0:8], small[:, 8:16], small[:, 16:24]
        shift1, scale1 = small[:, 24:32], small[:, 32:40]
        stats = small[:, 40:64].rearrange("p (t h s) -> p t h s", t=NT, h=2)
        moments = small[:, 64:68].rearrange("p (t s) -> p t s", t=NT)
        std, rstd = small[:, 68:70], small[:, 70:72]
        row_max, row_sum, row_inv = small[:, 72:74], small[:, 74:76], small[:, 76:78]
        pool_scale_c = small[:, 78:82]
        most_f, most_all = small[:, 82:83], small[:, 83:84]
        most_i = small[:, 84:85].bitcast(I32)
        one_bf = small[:, 85:86].bitcast(BF16)
        pick_rows = small[:, 86:102].bitcast(BF16)

        logits = view(attn_region, 0, 64).rearrange("p (t e) -> p t e", t=NT)
        top_v = view(attn_region, 64, 16).rearrange("p (t k) -> p t k", t=NT)
        top_i = view(attn_region, 80, 16, U32).rearrange("p (t k) -> p t k", t=NT)
        top_f = view(attn_region, 96, 16).rearrange("p (t k) -> p t k", t=NT)
        top_e = view(attn_region, 112, 8).rearrange("p (t k) -> p t k", t=NT)
        top_n, top_s, top_r = (view(attn_region, 120 + 2 * k, 2) for k in range(3))
        terms = view(attn_region, 128, NT * TOP_K * NE).rearrange("p (t k e) -> p t k e", t=NT, k=TOP_K)
        weight = view(attn_region, 384, NT * PADDED).rearrange("p (t e) -> p t e", t=NT)
        rank1 = view(attn_region, 452, NT * PADDED).rearrange("p (t e) -> p t e", t=NT)
        chosen = view(attn_region, 520, 32, BF16).rearrange("p (t e) -> p t e", t=NT)
        b_router_sb = router_w[0:1, KT, :]
        tri_bf = view(attn_region, 584, 64, BF16)
        chosen_f = terms[:, :, 0, :]
        weight_t = view(row_region, 2048, S, parts=NE)

        u2_parts = view(gate_region, 0, 3072, BF16).rearrange("p (m t n) -> p m t n", m=3, t=NT)
        y = view(gate_region, 3072, HALF)
        gate_min = view(gate_region, 3584, HALF)
        x_sel = view(feat_region, 0, 1024).rearrange("p (b k r) -> p b k r", b=2, k=KT)
        h = view(feat_region, 1024, HALF)
        h_t = view(feat_region, 1536, HALF).rearrange("p (c n) -> p c n", c=4)
        sig = view(acc_region, 0, HALF)
        up_c = view(acc_region, 512, HALF)
        scatter_t = view(ln_tok, 0, 1024).rearrange("p (b m t) -> p b m t", b=2, m=4)
        scatter = view(row_region, 0, NT * 192).rearrange("p (t r) -> p t r", t=NT)
        pick_tok = view(row_region, 384, 128, BF16).rearrange("p (b t r) -> p b t r", b=2, t=NT)
        pick_bias = view(row_region, 512, 64, BF16, parts=96).rearrange("p (b r) -> p b r", b=2)
        late_rank = view(row_region, 576, 2).rearrange("p (t r) -> p t r", t=NT)
        scaled_ident = view(row_region, 640, P)
        gate2_halves = view(row_region, 1024, HALF)
        y_late = view(ln_tok, 1024, HALF)

        ident = const[:, C_IDENT:C_IDENT + P]
        ranks = const[:, C_RANKS:C_RANKS + CAP]
        one = const[:, C_ONE:C_ONE + 1]
        eps = const[:, C_EPS:C_EPS + 1]

        bank = [ctx.enter_context(nc.psum_tensor(f"bank{b}", [P, HALF], F32)) for b in range(8)]
        T_BANKS = (4, 0, 1)
        G_BANK, U_BANK, Y_BANK, M_BANK = bank[4], bank[5], bank[6], bank[7]

        def slot(s):
            return ring[:, s * SLOT:(s + 1) * SLOT]

        def unit_view(u):
            s = slot(SLOT_OF[u])
            if u[0] in ("ada", "in"):
                n = HALF if u[0] == "ada" else IN_COLS[u[1]][1] - IN_COLS[u[1]][0]
                return s[:, 0:KT * n].rearrange("p (k n) -> p k n", k=KT)
            k = 2 if u[0] == "attn_out" else 4
            return s[:, 0:k * D].rearrange("p (k n) -> p k n", k=k)

        def unit_source(u):
            kind, j = u
            if kind == "ada":
                w = w_ada[0][:, HALF * j:HALF * (j + 1)]
            elif kind == "in":
                w = w_in[0][:, IN_COLS[j][0]:IN_COLS[j][1]]
            elif kind == "o":
                w = w_o[0][HALF * j:HALF * (j + 1), :]
            else:
                w = (w_attn_out if kind == "attn_out" else w_pool_out)[0]
            return w.rearrange("(k p) n -> p k n", p=P)

        expert_rows = [w[0].rearrange("e k n -> (e k) n") for w in (w_gate, w_up, w_down)]

        def expert_view(m):
            return slot(RING[m % SLOTS]).rearrange("p (k n) -> p k n", k=4)

        def expert_source(expert, k):
            rows = expert_rows[k // 2][bass.ds(expert * D + HALF * (k % 2), HALF), :]
            return rows.rearrange("(k p) n -> p k n", p=P)

        ld_x, ld_c, ld_const, ld_masks = [sem("ld_x0"), sem("ld_x1")], sem("ld_c"), sem("ld_const"), sem("ld_masks")
        ld_b_ada, ld_pos, ld_pool, ld_bias = sem("ld_b_ada"), sem("ld_pos"), sem("ld_pool"), sem("ld_bias")
        ld_ln1, ld_router, ld_b_down, ld_ln2 = sem("ld_ln1"), sem("ld_router"), sem("ld_b_down"), sem("ld_ln2")
        slot_landed = [sem(f"slot{s}_landed") for s in range(SLOTS)]
        pe_unit_used = sem("pe_unit_used")
        raw_cleared = sem("raw_cleared")
        pick_ready = sem("pick_ready")
        sig_c_ready = sem("sig_c_ready")
        dve_chain = sem("dve_chain")
        std_ready = sem("std_ready")
        moments_ready = sem("moments_ready")
        xn_ready = sem("xn_ready")
        xn_t_done = sem("xn_t_done")
        acc_ready = sem("acc_ready")
        acc_read = sem("acc_read")
        parts_ready = sem("parts_ready")
        ada_cols_ready = sem("ada_cols_ready")
        u_t_ready = sem("u_t_ready")
        row_ready = sem("row_ready")
        job_done = sem("job_done")
        job_read = sem("job_read")
        angle_ready = sem("angle_ready")
        trig_ready = sem("trig_ready")
        partner_done = sem("partner_done")
        rotated = sem("rotated")
        scores_done = sem("scores_done")
        scores_read = sem("scores_read")
        exp_ready = sem("exp_ready")
        probs_ready = sem("probs_ready")
        probs_t_done = sem("probs_t_done")
        probs_t_read = sem("probs_t_read")
        attn_done = sem("attn_done")
        attn_t_ready = sem("attn_t_ready")
        pool_chain = sem("pool_chain")
        pooled = sem("pooled")
        branch_done = sem("branch_done")
        merged = sem("merged")
        mix_done = sem("mix_done")
        u2_ready = sem("u2_ready")
        u2_t_done = sem("u2_t_done")
        u2_t_ready = sem("u2_t_ready")
        part_ready = sem("part_ready")
        rest_ready = sem("rest_ready")
        logits_done = sem("logits_done")
        top_ready = sem("top_ready")
        top_exp_ready = sem("top_exp_ready")
        weight_ready = sem("weight_ready")
        weight_t_done = sem("weight_t_done")
        weight_t_ready = sem("weight_t_ready")
        rank_done = sem("rank_done")
        tri_ready = sem("tri_ready")
        moe_chain = sem("moe_chain")
        moe_cleared = sem("moe_cleared")
        scaled_ready = sem("scaled_ready")
        b_down_ready = sem("b_down_ready")
        gate2_ready = sem("gate2_ready")
        seed_done = sem("seed_done")
        most_f_ready = sem("most_f_ready")
        most_all_ready = sem("most_all_ready")
        most_ready = sem("most_ready")
        picked = sem("picked")
        scatter_ready = sem("scatter_ready")
        gather_done = sem("gather_done")
        scatter_t_done = sem("scatter_t_done")
        misc_read = sem("misc_read")
        gate_done, up_done = sem("gate_done"), sem("up_done")
        gate_min_ready = sem("gate_min_ready")
        sig_ready = sem("sig_ready")
        h_ready = sem("h_ready")
        h_t_done = sem("h_t_done")
        y_ready = sem("y_ready")
        combined = sem("combined")
        final_chain = sem("final_chain")
        final_moments = sem("final_moments")
        final_std = sem("final_std")
        out_ready = sem("out_ready")
        out_written = sem("out_written")
        ovf_landed = sem("ovf_landed")
        ovf_pe, ovf_act, ovf_dve = sem("ovf_pe"), sem("ovf_act"), sem("ovf_dve")
        ovf_chain = sem("ovf_chain")

        jobs = [(("in", 1 + n // 2), n % 2) for n in range(6)]
        jobs += [(("in", 4), 0), (("in", 4), 1), (("in", 5), 0)]
        jobs += [(("in", 0), 0), (("in", 0), 1)]
        JOB_GATES = len(jobs)
        jobs += [(("in", 6 + n // 2), n % 2) for n in range(8)]
        JOB_POOL = len(jobs)

        def job_bank(n):
            return bank[6 + n % 2]

        def landed(eng, u):
            eng.wait_ge(slot_landed[SLOT_OF[u]], 16 * TURN_OF[u])

        block = ctx.enter_context(nc.Block())

        @block.sync
        def _(sp):
            for t in range(NT):
                sp.dma_start(x_tok[:, t, :], x[0, t * P:(t + 1) * P, :]).then_inc(ld_x[t], 16)

            def wait_used(u):
                if u[0] == "ada":
                    sp.wait_ge(acc_ready, u[1] + 1)
                elif u[0] == "in":
                    sp.wait_ge(job_done, max(n for n, (v, _) in enumerate(jobs) if v == u) + 1)
                elif u[0] == "o":
                    sp.wait_ge(mix_done, 2 * NT)
                else:
                    sp.wait_ge(branch_done, KT // 2)

            for n, u in enumerate(FRONT):
                if n >= FRONT_SLOTS:
                    wait_used(FRONT[n - FRONT_SLOTS])
                sp.dma_start(unit_view(u), unit_source(u)).then_inc(slot_landed[n % FRONT_SLOTS], 16)
            last_in_slot = {n % FRONT_SLOTS: u for n, u in enumerate(FRONT)}
            for m in range(SLOTS):
                if RING[m] < FRONT_SLOTS:
                    wait_used(last_in_slot[RING[m]])
                else:
                    sp.wait_ge(attn_done, 1)
                sp.dma_start(expert_view(m), expert_source(m // UNITS, m % UNITS)) \
                  .then_inc(slot_landed[RING[m]], 16)

            with sp.Fori(0, TURNS - 1) as i:
                for r in range(BODY * UNITS):
                    sp.wait_ge(pe_unit_used, i * (BODY * UNITS) + (r + 1))
                    k = SLOTS + r
                    sp.dma_start(expert_view(k), expert_source(i * BODY + k // UNITS, k % UNITS)) \
                      .then_inc(slot_landed[RING[k % SLOTS]], 16)
            for r in range(BODY * UNITS - SLOTS):
                sp.wait_ge(pe_unit_used, (TURNS - 1) * BODY * UNITS + r + 1)
                k = SLOTS + r
                sp.dma_start(expert_view(k), expert_source((TURNS - 1) * BODY + k // UNITS, k % UNITS)) \
                  .then_inc(slot_landed[RING[k % SLOTS]], 16)

            sp.wait_ge(most_ready, 1)
            most = sp.value_load(most_i[0:1, :], min_val=0, max_val=S)
            with sp.If(most > CAP):
                with sp.Fori(0, NE) as e:
                    sp.wait_ge(ovf_pe, e * (6 * CHUNKS) + 1)
                    for k in range(UNITS):
                        sp.dma_start(expert_view(k), expert_source(e, k)).then_inc(ovf_landed, 16)
            for t in range(NT):
                sp.wait_ge(out_ready, t + 1)
                sp.dma_start(out[0, t * P:(t + 1) * P, :], x_tok[:, t, :]).then_inc(out_written, 16)
            sp.wait_ge(out_written, 16 * NT)

        @block.scalar
        def _(act):
            act.dma_start(c_col, c[0].rearrange("(k p) -> p k", p=P), allow_slow_non_contiguous=True).then_inc(ld_c, 16)
            act.dma_start(const[:, :], const_table).then_inc(ld_const, 16)
            act.wait_ge(raw_cleared, 1)
            for m in range(3):
                act.dma_start(b_ada_raw[32 * m:32 * m + 12, :],
                              b_ada[0].rearrange("(j n) -> j n", j=12)).then_inc(ld_b_ada, 16)
            act.dma_start(pos_i, positions.to_broadcast([P, S])).then_inc(ld_pos, 16)
            act.dma_start(masks, mask_table.rearrange("p (g k n) -> p g k n", g=NG, k=2)).then_inc(ld_masks, 16)
            for m in range(3):
                for j, b in enumerate((b_gate, b_up)):
                    act.dma_start(bias_raw[32 * m:32 * m + NE, j, :], b[0]).then_inc(ld_bias, 16)
            act.dma_start(pool_w_sb, pool_w[0].rearrange("g c d -> c g d")).then_inc(ld_pool, 16)
            act.dma_start(pool_scale_c, pool_scale[0].rearrange("(g d) -> d g", g=PG),
                          allow_slow_non_contiguous=True).then_inc(ld_pool, 16)
            act.dma_start(router_w[:, 0:KT, :], w_router[0].rearrange("(k p) e -> p k e", p=P)) \
               .then_inc(ld_router, 16)
            act.dma_start(b_router_sb, b_router).then_inc(ld_router, 16)

            act.wait_ge(ld_c, 16)
            nc.scalar.activation(c_sig, c_col, ACT.Sigmoid).then_inc(sig_c_ready, 1)
            act.wait_ge(ld_const, 16)
            nc.scalar.activation(one_bf, one.to_broadcast([P, 2]), ACT.Copy)
            nc.scalar.activation(pick_rows, const[:, C_PICK:C_PICK + NE], ACT.Copy).then_inc(pick_ready, 1)
            for t in range(NT):
                act.wait_ge(moments_ready, t + 1)
                nc.scalar.activation(std[:, t:t + 1], moments[:, t, 1:2], ACT.Sqrt, bias=eps).then_inc(std_ready, 1)

            act.wait_ge(ada_cols_ready, 1)
            act.wait_ge(xn_t_done, 1)
            for k in range(KT):
                nc.scalar.activation(u_t[:, k, :], bank[k // 2][:, (k % 2) * S:(k % 2 + 1) * S], ACT.Identity,
                                     bias=shift1[:, k:k + 1], scale=scale1[:, k:k + 1]).then_inc(u_t_ready, 1)

            def row(j):
                act.wait_ge(acc_read, j + 1)
                r = j - 4
                nc.scalar.activation(ada_rows[:, r // 2, (r % 2) * HALF:(r % 2 + 1) * HALF], bank[5][:, :],
                                     ACT.Copy, bias=0.0 if r // 2 == 1 else 1.0).then_inc(row_ready, 1)

            def job(n):
                act.wait_ge(job_done, n + 1)
                src = job_bank(n)[:, :]
                pair = src.rearrange("p (j t) -> p j t", j=2)
                if n < 6:
                    nc.scalar.activation(qk[:, 2 * n:2 * n + 2, :], pair, ACT.Copy).then_inc(job_read, 1)
                elif n < 8:
                    nc.scalar.activation(v_tok[:, n - 6, 0:HALF], src, ACT.Copy).then_inc(job_read, 1)
                elif n == 8:
                    nc.scalar.activation(v_tok[:, :, HALF:ATTN_WIDTH], pair, ACT.Copy).then_inc(job_read, 1)
                elif n < JOB_GATES:
                    j = 2 * (n - 9)
                    nc.scalar.activation(xp_t[:, j:j + 2, :], pair, ACT.Copy).then_inc(job_read, 1)
                elif n < JOB_POOL:
                    j = 2 * (n - JOB_GATES)
                    if j == 0:
                        act.wait_ge(parts_ready, 3)
                    if j == 12:
                        act.wait_ge(pooled, 1)
                    nc.scalar.activation(gates[:, j:j + 2, :], pair, ACT.Sigmoid).then_inc(job_read, 1)
                else:
                    for j in range(2):
                        g = 2 * (n - JOB_POOL) + j
                        last = nc.scalar.activation(xp_t[:, g, :], pair[:, j, :], ACT.Copy,
                                                    scale=pool_scale_c[:, g:g + 1])
                    last.then_inc(job_read, 1)

            for n in range(2):
                job(n)
            for k, table in enumerate((sin, cos)):
                act.wait_ge(angle_ready, k + 1)
                nc.scalar.activation(table, rot_tmp[:, k, :], ACT.Sin).then_inc(trig_ready, 1)
            for n in range(2, 7):
                job(n)
            row(4)
            for n in (7, 8):
                job(n)
            row(5)
            for n in (9, 10):
                job(n)
            row(6)
            for s in range(HEAD_SLOTS):
                for t in range(NT):
                    act.wait_ge(scores_read, 2 * s + t + 1)
                    part = probs[:, 384 * t:384 * t + 384 * (t + 1)]
                    nc.scalar.activation(part, part, ACT.Exp, bias=row_max[:, t:t + 1],
                                         accum_out=row_sum[:, t:t + 1]).then_inc(exp_ready, 1)
                job(JOB_GATES + 2 * s)
                for g in range(NG):
                    act.wait_ge(probs_t_done, NG * s + g + 1)
                    nc.scalar.activation(probs_t[:, g, :], bank[T_BANKS[g]][:, 0:384], ACT.Copy) \
                      .then_inc(probs_t_read, 1)
                if s >= 1:
                    row(6 + s)
                job(JOB_GATES + 2 * s + 1)
            act.wait_ge(attn_done, 1)
            nc.scalar.activation(attn_t, bank[3][:, :].rearrange("p (j t) -> p j t", j=2), ACT.Copy) \
              .then_inc(attn_t_ready, 1)
            act.wait_ge(ld_pool, 32)
            for n in range(2):
                job(JOB_POOL + n)
            row(10)
            row(11)
            act.wait_ge(pooled, 1)
            act.wait_ge(merged, KT // 2)
            for r, w in enumerate((ln1_g, ln1_b)):
                act.dma_start(ln_rows[:, r, :], w.to_broadcast([P, D])).then_inc(ld_ln1, 16)
            act.dma_start(b_down_sb, b_down[0]).then_inc(ld_b_down, 16)
            for t in range(NT):
                for k in range(2):
                    act.wait_ge(moments_ready, 2 + 2 * t + k + 1)
                    nc.scalar.activation(std[:, t:t + 1], moments[:, t, 1:2], ACT.Sqrt, bias=eps) \
                      .then_inc(std_ready, 1)
            nc.scalar.activation(tri_bf, const[:, C_TRI:C_TRI + P], ACT.Copy).then_inc(tri_ready, 1)
            nc.scalar.activation(scaled_ident, ident, ACT.Copy, scale=DN_ALPHA).then_inc(scaled_ready, 1)
            act.wait_ge(mix_done, 2 * NT)
            for t in range(NT):
                act.wait_ge(u2_t_done, t + 1)
                for b in range(2):
                    nc.scalar.activation(u_t[:, 4 * b:4 * b + 4, t * P:(t + 1) * P],
                                         bank[(6, 0)[t] + b][:, :].rearrange("p (k t) -> p k t", k=4),
                                         ACT.Copy).then_inc(u2_t_ready, 1)
                nc.scalar.activation(u2_parts[:, 0, t, :], u2[:, t, :], ACT.Copy).then_inc(part_ready, 1)
            act.wait_ge(u2_ready, NT)
            for r, w in enumerate((ln2_g, ln2_b)):
                act.dma_start(ln_rows[:, r, :], w.to_broadcast([P, D])).then_inc(ld_ln2, 16)
            for t in range(NT):
                act.wait_ge(top_ready, t + 1)
                nc.scalar.activation(top_e[:, t, :], top_v[:, t, 0:TOP_K], ACT.Exp, bias=top_n[:, t:t + 1],
                                     accum_out=top_s[:, t:t + 1]).then_inc(top_exp_ready, 1)
            for m in (1, 2):
                for t in range(NT):
                    act.wait_ge(rest_ready, NT * (m - 1) + t + 1)
                    nc.scalar.activation(u2_parts[:, m, t, :], u2[:, t, :], ACT.Copy).then_inc(part_ready, 1)
            act.wait_ge(weight_t_done, 1)
            nc.scalar.activation(weight_t, M_BANK[0:NE, 0:S], ACT.Copy).then_inc(weight_t_ready, 1)
            for hf in range(2):
                last = nc.scalar.activation(gate2_halves[hf * CAP:(hf + 1) * CAP, :],
                                            ada_rows[hf * CAP:(hf + 1) * CAP, 3, hf * HALF:(hf + 1) * HALF], ACT.Copy)
            last.then_inc(gate2_ready, 1)

            act.wait_ge(gather_done, 1)
            nc.scalar.activation(x_sel[:, 0], M_BANK[:, :].rearrange("p (k r) -> p k r", k=KT), ACT.Copy) \
              .then_inc(misc_read, 1)
            with act.Fori(0, TURNS) as i:
                for j in range(BODY):
                    act.wait_ge(gather_done, i * BODY + (j + 2))
                    nc.scalar.activation(x_sel[:, (j + 1) % 2], M_BANK[:, :].rearrange("p (k r) -> p k r", k=KT),
                                         ACT.Copy).then_inc(misc_read, 1)
                    act.wait_ge(scatter_t_done, i * BODY + (j + 1))
                    nc.scalar.activation(scatter_t[:, j % 2], M_BANK[:, :].rearrange("p (m t) -> p m t", m=4),
                                         ACT.Copy).then_inc(misc_read, 1)
                    act.wait_ge(gate_min_ready, i * BODY + (j + 1))
                    nc.scalar.activation(sig, gate_min, ACT.Sigmoid, scale=SWIGLU_ALPHA).then_inc(sig_ready, 1)
                    act.wait_ge(h_t_done, i * BODY + (j + 1))
                    nc.scalar.activation(h_t, M_BANK[:, :].rearrange("p (c n) -> p c n", c=4), ACT.Copy) \
                      .then_inc(misc_read, 1)

            act.wait_ge(most_ready, 1)
            most = act.value_load(most_i[0:1, :], min_val=0, max_val=S)
            with act.If(most > CAP):
                with act.Fori(0, NE) as e:
                    for n in range(CHUNKS):
                        act.wait_ge(ovf_pe, e * (6 * CHUNKS) + (6 * n + 2))
                        nc.scalar.activation(x_sel[:, 0], M_BANK[:, :].rearrange("p (k r) -> p k r", k=KT),
                                             ACT.Copy).then_inc(ovf_act, 1)
                        act.wait_ge(ovf_pe, e * (6 * CHUNKS) + (6 * n + 3))
                        nc.scalar.activation(scatter_t[:, 0], M_BANK[:, :].rearrange("p (m t) -> p m t", m=4),
                                             ACT.Copy).then_inc(ovf_act, 1)
                        act.wait_ge(ovf_dve, e * (4 * CHUNKS) + (4 * n + 2))
                        nc.scalar.activation(sig, gate_min, ACT.Sigmoid, scale=SWIGLU_ALPHA).then_inc(ovf_act, 1)
                        act.wait_ge(ovf_pe, e * (6 * CHUNKS) + (6 * n + 5))
                        nc.scalar.activation(h_t, M_BANK[:, :].rearrange("p (c n) -> p c n", c=4), ACT.Copy) \
                          .then_inc(ovf_act, 1)
            for t in range(NT):
                act.wait_ge(final_moments, t + 1)
                nc.scalar.activation(std[:, t:t + 1], moments[:, t, 1:2], ACT.Sqrt, bias=eps).then_inc(final_std, 1)

        @block.vector
        def _(dve):
            counts = {}

            def step(ins, s=dve_chain):
                counts[s.name] = counts.get(s.name, 0) + 1
                ins.then_inc(s, 1)
                dve.wait_ge(s, counts[s.name])

            def split(raw, parts):
                step(nc.vector.tensor_copy(parts, raw))
                for drop in (C_DROP1, C_DROP2):
                    step(nc.vector.scalar_tensor_tensor(out=raw, in0=parts, scalar=const[0:96, drop:drop + 1],
                                                        in1=raw, op0=ALU.mult, op1=ALU.add))
                    step(nc.vector.tensor_copy(parts, raw), parts_ready if drop == C_DROP2 else dve_chain)

            dve.wait_ge(sig_c_ready, 1)
            step(nc.vector.tensor_tensor(c_silu, c_col, c_sig, ALU.mult))

            def norm(src, dst, t, n_std):
                for hf in range(2):
                    step(nc.vector.bn_stats(stats[:, t, hf, :], src[:, t, hf * HALF:(hf + 1) * HALF]))
                step(nc.vector.bn_aggr(moments[:, t, :], stats[:, t]), moments_ready)
                dve.wait_ge(std_ready, n_std)
                step(nc.vector.reciprocal(rstd[:, t:t + 1], std[:, t:t + 1]))
                return nc.vector.tensor_scalar(dst[:, t, :], src[:, t, :], moments[:, t, 0:1], rstd[:, t:t + 1],
                                               ALU.subtract, ALU.mult)

            def scaled_norm(src, dst, t, n_std, scale_row, shift_row, s=dve_chain):
                step(nc.vector.bn_aggr(moments[:, t, :], stats[:, t]), moments_ready)
                step(nc.vector.scalar_tensor_tensor(out=dst[:, t, :], in0=src[:, t, :], scalar=moments[:, t, 0:1],
                                                    in1=scale_row, op0=ALU.subtract, op1=ALU.mult))
                dve.wait_ge(std_ready, n_std)
                step(nc.vector.reciprocal(rstd[:, t:t + 1], std[:, t:t + 1]))
                step(nc.vector.scalar_tensor_tensor(out=dst[:, t, :], in0=dst[:, t, :], scalar=rstd[:, t:t + 1],
                                                    in1=shift_row, op0=ALU.mult, op1=ALU.add), s)

            for t in range(NT):
                dve.wait_ge(ld_x[t], 16)
                norm(x_tok, xn, t, t + 1).then_inc(xn_ready, 1)

            def ada(j):
                if j >= 2:
                    dve.wait_ge(acc_read, j - 1)
                landed(dve, ("ada", j))
                w, acc = unit_view(("ada", j)), ada_acc[:, j % 2, :]
                step(nc.vector.tensor_scalar(acc, w[:, 0, :], c_silu[:, 0:1], None, ALU.mult))
                for k in range(1, KT):
                    ins = nc.vector.scalar_tensor_tensor(out=acc, in0=w[:, k, :], scalar=c_silu[:, k:k + 1],
                                                         in1=acc, op0=ALU.mult, op1=ALU.add)
                    if k < KT - 1:
                        step(ins)
                ins.then_inc(acc_ready, 1)

            ada(0)
            dve.wait_ge(ld_const, 16)
            dve.wait_ge(ld_b_ada, 48)
            split(b_ada_raw, ada_parts[:, :])
            for j in range(1, 4):
                ada(j)
            dve.wait_ge(acc_read, 4)
            nc.vector.tensor_copy(shift1, bank[4][:, 0:8])
            nc.vector.tensor_scalar(scale1, bank[4][:, 8:16], 1.0, None, ALU.add).then_inc(ada_cols_ready, 1)

            dve.wait_ge(ld_pos, 16)
            step(nc.vector.tensor_copy(angle, pos_i))
            step(nc.vector.tensor_scalar(angle, angle, const[:, C_FREQ:C_FREQ + 1], None, ALU.mult))
            for k in range(2):
                r = rot_tmp[:, k, :]
                step(nc.vector.tensor_scalar(turns, angle, 1.0 / (2.0 * math.pi), 0.25 * k, ALU.mult, ALU.add))
                step(nc.vector.tensor_scalar(turns, turns, ROUND, None, ALU.add))
                step(nc.vector.tensor_scalar(turns, turns, -ROUND, None, ALU.add))
                src = angle
                for part in TWO_PI_PARTS:
                    step(nc.vector.scalar_tensor_tensor(out=r, in0=turns, scalar=-part, in1=src,
                                                        op0=ALU.mult, op1=ALU.add))
                    src = r
                step(nc.vector.tensor_scalar(r, r, 0.5 * math.pi * k, None, ALU.add))
                step(nc.vector.tensor_scalar(r, r, 3.1415925, -3.1415925, ALU.min, ALU.max), angle_ready)

            def rotate(n):
                dve.wait_ge(trig_ready, 2)
                dve.wait_ge(partner_done, n + 1)
                pair, part = qk[:, 2 * n:2 * n + 2, :], bank[2 + n % 2][:, :].rearrange("p (j t) -> p j t", j=2)
                cos2, sin2 = (a.unsqueeze(1).to_broadcast([P, 2, S]) for a in (cos, sin))
                step(nc.vector.tensor_tensor(rot_tmp, part, sin2, ALU.mult))
                step(nc.vector.tensor_tensor(pair, pair, cos2, ALU.mult))
                step(nc.vector.tensor_tensor(pair, pair, rot_tmp, ALU.add), rotated)

            for n in range(2):
                rotate(n)
            ada(4)
            for n in (2, 3):
                rotate(n)
            ada(5)
            for n in (4, 5):
                rotate(n)
            dve.wait_ge(ld_bias, 96)
            split(bias_raw[:, 0, :], bias_parts[:, 0, :])
            ada(6)
            split(bias_raw[:, 1, :], bias_parts[:, 1, :])
            ada(7)

            dve.wait_ge(ld_masks, 16)
            for s in range(HEAD_SLOTS):
                for t in range(NT):
                    dve.wait_ge(scores_done, 2 * s + t + 1)
                    if t == 0:
                        part = probs[:, 0:384]
                        step(nc.vector.scalar_tensor_tensor(
                            out=part.rearrange("p (g n) -> p g n", g=NG),
                            in0=bank[0][:, 0:384].rearrange("p (g n) -> p g n", g=NG), scalar=HEAD_DIM ** -0.5,
                            in1=masks[:, :, 1, :], op0=ALU.mult, op1=ALU.add))
                    else:
                        part = probs[:, 384:1152]
                        flat = masks.rearrange("p g k n -> p (g k n)")
                        step(nc.vector.scalar_tensor_tensor(
                            out=part[:, 0:512], in0=bank[1][:, :], scalar=HEAD_DIM ** -0.5,
                            in1=flat[:, 0:512], op0=ALU.mult, op1=ALU.add))
                        step(nc.vector.scalar_tensor_tensor(
                            out=part[:, 512:768], in0=bank[2][:, 0:256], scalar=HEAD_DIM ** -0.5,
                            in1=flat[:, 512:768], op0=ALU.mult, op1=ALU.add))
                    step(nc.vector.tensor_reduce(row_max[:, t:t + 1], part, AX.X, ALU.max, negate=True),
                         scores_read)
                for t in range(NT):
                    part = probs[:, 384 * t:384 * t + 384 * (t + 1)]
                    dve.wait_ge(exp_ready, 2 * s + t + 1)
                    step(nc.vector.reciprocal(row_inv[:, t:t + 1], row_sum[:, t:t + 1]))
                    step(nc.vector.tensor_scalar(part, part, row_inv[:, t:t + 1], None, ALU.mult), probs_ready)
                ada(8 + s)

            for n in range(KT // 2):
                dve.wait_ge(job_read, JOB_POOL + 2)
                dve.wait_ge(branch_done, n + 1)
                gp, ga = gates[:, 2 * n:2 * n + 2, :], gates[:, KT + 2 * n:KT + 2 * n + 2, :]
                bp, ba = (bank[b + n % 2][:, :].rearrange("p (j t) -> p j t", j=2) for b in (6, 0))
                step(nc.vector.tensor_tensor(gp, gp, bp, ALU.mult))
                step(nc.vector.tensor_tensor(ga, ga, ba, ALU.mult))
                step(nc.vector.tensor_tensor(gp, gp, ga, ALU.add), merged)

            dve.wait_ge(row_ready, 8)
            for t in range(NT):
                for hf in range(2):
                    cols = slice(hf * HALF, (hf + 1) * HALF)
                    dve.wait_ge(mix_done, 2 * t + hf + 1)
                    step(nc.vector.tensor_tensor(xn[:, t, cols], bank[2 + 2 * t + hf][:, :], ada_rows[:, 0, cols],
                                                 ALU.mult))
                    step(nc.vector.scalar_tensor_tensor(out=x_tok[:, t, cols], in0=x_tok[:, t, cols],
                                                        scalar=DN_ALPHA, in1=xn[:, t, cols],
                                                        op0=ALU.mult, op1=ALU.add))
                    step(nc.vector.bn_stats(stats[:, t, hf, :], x_tok[:, t, cols]))
                dve.wait_ge(ld_ln1, 32)
                scaled_norm(x_tok, x_tok, t, 2 + 2 * t + 1, ln_rows[:, 0, :], ln_rows[:, 1, :])
                for hf in range(2):
                    step(nc.vector.bn_stats(stats[:, t, hf, :], x_tok[:, t, hf * HALF:(hf + 1) * HALF]))
                scaled_norm(x_tok, u2, t, 2 + 2 * t + 2, ada_rows[:, 2, :], ada_rows[:, 1, :], u2_ready)

            for t in range(NT):
                dve.wait_ge(logits_done, t + 1)
                step(nc.vector.tensor_copy(logits[:, t, :], bank[2 + t][:, 0:NE]), moe_chain)
                step(nc.vector.max(top_v[:, t, :], logits[:, t, :]), moe_chain)
                step(nc.vector.tensor_scalar(top_n[:, t:t + 1], top_v[:, t, 0:1], -1.0, None, ALU.mult), top_ready)
                step(nc.vector.max_index(top_i[:, t, :], top_v[:, t, :], logits[:, t, :]), moe_chain)
                step(nc.vector.tensor_copy(top_f[:, t, :], top_i[:, t, :]), moe_chain)
            step(nc.vector.memset(weight[:, :, NE:PADDED], 0.0), moe_chain)
            step(nc.vector.memset(rank1[:, :, NE:PADDED], 0.0), moe_chain)
            for t in range(NT):
                dve.wait_ge(top_exp_ready, t + 1)
                step(nc.vector.reciprocal(top_r[:, t:t + 1], top_s[:, t:t + 1]), moe_chain)
                step(nc.vector.tensor_scalar(top_e[:, t, :], top_e[:, t, :], top_r[:, t:t + 1], None, ALU.mult),
                     moe_chain)
                for k in range(TOP_K):
                    step(nc.vector.tensor_scalar(terms[:, t, k, :], const[:, C_EXPERTS:C_EXPERTS + NE],
                                                 top_f[:, t, k:k + 1], top_e[:, t, k:k + 1],
                                                 ALU.is_equal, ALU.mult), moe_chain)
                step(nc.vector.tensor_reduce(weight[:, t, 0:NE], terms[:, t].rearrange("p k e -> p e k"),
                                             AX.X, ALU.add), moe_chain)
            step(nc.vector.tensor_scalar(chosen, weight[:, :, 0:NE], 0.0, None, ALU.is_gt), weight_ready)
            step(nc.vector.tensor_scalar(chosen_f, weight[:, :, 0:NE], 0.0, None, ALU.is_gt), moe_chain)
            dve.wait_ge(rank_done, 1)
            step(nc.vector.scalar_tensor_tensor(out=rank1[:, :, 0:NE],
                                                in0=Y_BANK[:, 0:NT * NE].rearrange("p (t e) -> p t e", t=NT),
                                                scalar=1.0, in1=chosen_f, op0=ALU.add, op1=ALU.mult), moe_chain)

            def pick_expert(e, b):
                col = rank1[:, :, bass.ds(e, 1)].to_broadcast([P, NT, CAP])
                return nc.vector.tensor_tensor(pick_tok[:, b], ranks.unsqueeze(1).to_broadcast([P, NT, CAP]),
                                               col, ALU.is_equal)

            def pick_biases(e, b):
                col = const[0:96, C_PICK:C_PICK + NE + 1][:, bass.ds(e, 1)].to_broadcast([96, CAP])
                return nc.vector.tensor_scalar(pick_bias[:, b, :], col, 1.0, None, ALU.mult)

            dve.wait_ge(moe_cleared, 1)
            pick_biases(0, 0)
            pick_expert(0, 0).then_inc(picked, 1)
            pick_expert(1, 1).then_inc(picked, 1)
            step(nc.vector.tensor_tensor(scatter[:, :, 64:128], ranks.unsqueeze(1).to_broadcast([P, NT, CAP]),
                                         rank1[:, :, 0:1].to_broadcast([P, NT, CAP]), ALU.is_equal), moe_chain)
            nc.vector.tensor_tensor(scatter[:, :, 64:128], scatter[:, :, 64:128],
                                    weight[:, :, 0:1].to_broadcast([P, NT, CAP]), ALU.mult).then_inc(scatter_ready, 1)
            step(nc.vector.tensor_reduce(most_f, rank1[:, :, 0:NE], AX.XY, ALU.max), most_f_ready)

            dve.wait_ge(gate2_ready, 1)
            base = counts[moe_chain.name]
            own = 3
            with dve.Fori(0, TURNS) as i:
                for j in range(BODY):
                    def chain(ins, k):
                        ins.then_inc(moe_chain, 1)
                        dve.wait_ge(moe_chain, i * (BODY * own) + (base + j * own + k + 1))

                    dve.wait_ge(gate_done, i * BODY + (j + 1))
                    nc.vector.tensor_scalar(gate_min, G_BANK[:, :], SWIGLU_LIMIT, None, ALU.min) \
                      .then_inc(gate_min_ready, 1)
                    pick_biases(i * BODY + (j + 1), (j + 1) % 2)
                    pick_expert(i * BODY + (j + 2), j % 2).then_inc(picked, 1)
                    dve.wait_ge(scatter_t_done, i * BODY + (j + 1))
                    chain(nc.vector.tensor_tensor(
                        scatter[:, :, 64:128], ranks.unsqueeze(1).to_broadcast([P, NT, CAP]),
                        rank1[:, :, bass.ds(i * BODY + (j + 1), 1)].to_broadcast([P, NT, CAP]), ALU.is_equal), 0)
                    nc.vector.tensor_tensor(
                        scatter[:, :, 64:128], scatter[:, :, 64:128],
                        weight[:, :, bass.ds(i * BODY + (j + 1), 1)].to_broadcast([P, NT, CAP]), ALU.mult) \
                      .then_inc(scatter_ready, 1)
                    dve.wait_ge(up_done, i * BODY + (j + 1))
                    chain(nc.vector.tensor_scalar(up_c, U_BANK[:, :], SWIGLU_LIMIT, -SWIGLU_LIMIT,
                                                  ALU.min, ALU.max), 1)
                    dve.wait_ge(gate_min_ready, i * BODY + (j + 1))
                    chain(nc.vector.scalar_tensor_tensor(out=up_c, in0=up_c, scalar=1.0, in1=gate_min,
                                                         op0=ALU.add, op1=ALU.mult), 2)
                    dve.wait_ge(sig_ready, i * BODY + (j + 1))
                    nc.vector.tensor_tensor(h, up_c, sig, ALU.mult).then_inc(h_ready, 1)
                    dve.wait_ge(pe_unit_used, i * (BODY * UNITS) + UNITS * (j + 1))
                    nc.vector.tensor_tensor(y, Y_BANK[:, :], gate2_halves, ALU.mult).then_inc(y_ready, 1)

            dve.wait_ge(most_ready, 1)
            most = dve.value_load(most_i[0:1, :], min_val=0, max_val=S)
            own_ovf = 6
            with dve.If(most > CAP):
                with dve.Fori(0, NE) as e:
                    for n in range(CHUNKS):
                        k = [0]

                        def chain(ins):
                            k[0] += 1
                            ins.then_inc(ovf_chain, 1)
                            dve.wait_ge(ovf_chain, e * (CHUNKS * own_ovf) + (n * own_ovf + k[0]))

                        chain(nc.vector.tensor_scalar(late_rank, rank1[:, :, bass.ds(e, 1)], -float(CAP * (n + 1)),
                                                      None, ALU.add))
                        chain(pick_biases(e, 0))
                        chain(nc.vector.tensor_tensor(pick_tok[:, 0], ranks.unsqueeze(1).to_broadcast([P, NT, CAP]),
                                                      late_rank.to_broadcast([P, NT, CAP]), ALU.is_equal))
                        chain(nc.vector.tensor_copy(scatter[:, :, 64:128], pick_tok[:, 0]))
                        nc.vector.tensor_tensor(scatter[:, :, 64:128], scatter[:, :, 64:128],
                                                weight[:, :, bass.ds(e, 1)].to_broadcast([P, NT, CAP]),
                                                ALU.mult).then_inc(ovf_dve, 1)
                        dve.wait_ge(ovf_pe, e * (6 * CHUNKS) + (6 * n + 4))
                        nc.vector.tensor_scalar(gate_min, G_BANK[:, :], SWIGLU_LIMIT, None, ALU.min) \
                          .then_inc(ovf_dve, 1)
                        chain(nc.vector.tensor_scalar(up_c, U_BANK[:, :], SWIGLU_LIMIT, -SWIGLU_LIMIT,
                                                      ALU.min, ALU.max))
                        dve.wait_ge(ovf_dve, e * (4 * CHUNKS) + (4 * n + 2))
                        chain(nc.vector.scalar_tensor_tensor(out=up_c, in0=up_c, scalar=1.0, in1=gate_min,
                                                             op0=ALU.add, op1=ALU.mult))
                        dve.wait_ge(ovf_act, e * (4 * CHUNKS) + (4 * n + 3))
                        nc.vector.tensor_tensor(h, up_c, sig, ALU.mult).then_inc(ovf_dve, 1)
                        dve.wait_ge(ovf_pe, e * (6 * CHUNKS) + (6 * n + 6))
                        nc.vector.tensor_tensor(y_late, Y_BANK[:, :], gate2_halves, ALU.mult).then_inc(ovf_dve, 1)
                        assert k[0] == own_ovf

            n_final = [0]

            def final(ins):
                n_final[0] += 1
                ins.then_inc(final_chain, 1)
                dve.wait_ge(final_chain, n_final[0])

            dve.wait_ge(ld_ln2, 32)
            for t in range(NT):
                dve.wait_ge(combined, t + 1)
                for hf in range(2):
                    final(nc.vector.bn_stats(stats[:, t, hf, :], bank[2 * t + hf][:, :]))
                nc.vector.bn_aggr(moments[:, t, :], stats[:, t]).then_inc(final_moments, 1)
                dve.wait_ge(final_moments, t + 1)
                for hf in range(2):
                    cols = slice(hf * HALF, (hf + 1) * HALF)
                    final(nc.vector.scalar_tensor_tensor(out=x_tok[:, t, cols], in0=bank[2 * t + hf][:, :],
                                                         scalar=moments[:, t, 0:1], in1=ln_rows[:, 0, cols],
                                                         op0=ALU.subtract, op1=ALU.mult))
                dve.wait_ge(final_std, t + 1)
                final(nc.vector.reciprocal(rstd[:, t:t + 1], std[:, t:t + 1]))
                nc.vector.scalar_tensor_tensor(out=x_tok[:, t, :], in0=x_tok[:, t, :], scalar=rstd[:, t:t + 1],
                                               in1=ln_rows[:, 1, :], op0=ALU.mult, op1=ALU.add) \
                  .then_inc(out_ready, 1)

        @block.gpsimd
        def _(pool):
            count = [0]

            def step(ins):
                count[0] += 1
                ins.then_inc(pool_chain, 1)
                pool.wait_ge(pool_chain, count[0])

            nc.gpsimd.memset(b_ada_raw, 0.0).then_inc(raw_cleared, 1)
            pool.wait_ge(job_read, JOB_GATES)
            src = xp_t
            for k in range(PG):
                dst = (mixed, pool_tmp)[k % 2]
                if k == 1:
                    pool.wait_ge(ld_bias, 96)
                step(nc.gpsimd.tensor_copy(dst[:, k:PG, 0:1 << k], src[:, k:PG, 0:1 << k]))
                step(nc.gpsimd.tensor_tensor(dst[:, k:PG, 1 << k:S], src[:, k:PG, 1 << k:S],
                                             src[:, k:PG, 0:S - (1 << k)], ALU.add))
                src = dst
            for g, w in enumerate(POOL_WINDOWS):
                sums = (mixed, pool_tmp)[g % 2]
                rcnt = const[:, C_RCNT + 16 * g:C_RCNT + 16 * g + 16]
                step(nc.gpsimd.tensor_tensor(mixed[:, g, 0:16], sums[:, g, 0:16], rcnt, ALU.mult))
                step(nc.gpsimd.tensor_scalar(mixed[:, g, 16:S], sums[:, g, 16:S], 1.0 / w, None, ALU.mult))
            nc.gpsimd.tensor_tensor(mixed, mixed, xp_t, ALU.subtract).then_inc(pooled, 1)

            pool.wait_ge(moments_ready, 2 + 2 * NT - 1)
            nc.gpsimd.memset(scatter, 0.0).then_inc(moe_cleared, 1)
            pool.wait_ge(ld_b_down, 16)
            pool.wait_ge(row_ready, 8)
            nc.gpsimd.tensor_tensor(b_down_sb, b_down_sb, ada_rows[0:NE, 3, :], ALU.mult).then_inc(b_down_ready, 1)
            for m in range(2):
                for t in range(NT):
                    pool.wait_ge(part_ready, NT * m + t + 1)
                    pool.wait_ge(u2_t_done, t + 1)
                    nc.gpsimd.tensor_tensor(u2[:, t, :], u2[:, t, :], u2_parts[:, m, t, :], ALU.subtract) \
                      .then_inc(rest_ready, 1)
            pool.wait_ge(part_ready, 3 * NT)
            nc.gpsimd.memset(scatter_t[:, 1], 0.0)
            pool.wait_ge(seed_done, 1)
            nc.gpsimd.memset(y, 0.0).then_inc(y_ready, 1)
            pool.wait_ge(most_f_ready, 1)
            nc.gpsimd.partition_all_reduce(most_all, most_f, P, bass.bass_isa.ReduceOp.max).then_inc(most_all_ready, 1)
            pool.wait_ge(most_all_ready, 1)
            nc.gpsimd.tensor_copy(most_i, most_all).then_inc(most_ready, 1)

        @block.tensor
        def _(pe):
            pe.wait_ge(ld_const, 16)
            for t in range(NT):
                pe.wait_ge(xn_ready, t + 1)
                for k in range(KT):
                    last = nc.tensor.transpose(bank[k // 2][:, (k % 2) * S + t * P:(k % 2) * S + (t + 1) * P],
                                               xn[:, t, k * P:(k + 1) * P], ident)
            last.then_inc(xn_t_done, 1)

            pe.wait_ge(pick_ready, 1)
            pe.wait_ge(parts_ready, 1)
            for j in range(4):
                pe.wait_ge(acc_ready, j + 1)
                for q in range(4):
                    col = bank[4][:, 4 * j + q:4 * j + q + 1]
                    nc.tensor.matmul(col, ada_acc[:, j % 2, q * P:(q + 1) * P], one, start=True, stop=False)
                    last = nc.tensor.matmul(col, ada_parts[:, q * P:(q + 1) * P], pick_rows[0:96, j:j + 1],
                                            start=False, stop=True)
                last.then_inc(acc_read, 1)

            def row(j):
                pe.wait_ge(acc_ready, j + 1)
                if j > 4:
                    pe.wait_ge(row_ready, j - 4)
                nc.tensor.matmul(bank[5][:, :], one.to_broadcast([P, P]), ada_acc[:, j % 2, :],
                                 start=True, stop=False)
                nc.tensor.matmul(bank[5][:, :], pick_rows[0:96, j:j + 1].to_broadcast([96, P]), ada_parts[:, :],
                                 start=False, stop=True).then_inc(acc_read, 1)

            def job(n):
                u, part = jobs[n]
                w, dst = unit_view(u), job_bank(n)
                if n >= 2:
                    pe.wait_ge(job_read, n - 1)
                landed(pe, u)
                if u[1] in (4, 5):
                    for t in ((part,) if u[1] == 4 else range(NT)):
                        cols = slice(0, HALF) if u[1] == 4 else slice(t * S, (t + 1) * S)
                        for k in range(KT):
                            last = nc.tensor.matmul(dst[:, cols], u_t[:, k, t * P:(t + 1) * P], w[:, k, :],
                                                    start=k == 0, stop=k == KT - 1)
                else:
                    for q in range(2):
                        f = 2 * part + q
                        for k in range(KT):
                            last = nc.tensor.matmul(dst[:, q * S:(q + 1) * S], w[:, k, f * P:(f + 1) * P],
                                                    u_t[:, k, :], start=k == 0, stop=k == KT - 1)
                last.then_inc(job_done, 1)

            def partner(n):
                pe.wait_ge(job_read, n + 1)
                if n >= 2:
                    pe.wait_ge(rotated, n - 1)
                nc.tensor.matmul(bank[2 + n % 2][:, :], const[:, C_PERM:C_PERM + P],
                                 qk[:, 2 * n:2 * n + 2, :].rearrange("p j t -> p (j t)"),
                                 start=True, stop=True).then_inc(partner_done, 1)

            pe.wait_ge(u_t_ready, KT)
            job(0)
            for n in range(1, 7):
                job(n)
                partner(n - 1)
            row(4)
            job(7)
            job(8)
            row(5)
            job(9)
            job(10)
            row(6)

            pe.wait_ge(rotated, QT)
            for s in range(HEAD_SLOTS):
                for t in range(NT):
                    for g in range(NG):
                        head = g * HEAD_SLOTS + s
                        rows = slice(HEAD_DIM * (head % 2), HEAD_DIM * (head % 2 + 1))
                        q = qk[rows, head // 2, t * P:(t + 1) * P]
                        keys = qk[rows, QT + head // 2, 0:(t + 1) * P]
                        dst = bank[0][:, g * P:(g + 1) * P] if t == 0 else \
                            bank[1 + g // 2][:, (g % 2) * S:(g % 2 + 1) * S]
                        last = nc.tensor.matmul(dst, q, keys, start=True, stop=True)
                    last.then_inc(scores_done, 1)
                job(JOB_GATES + 2 * s)
                pe.wait_ge(probs_ready, 2 * (s + 1))
                for g in range(NG):
                    dst = bank[T_BANKS[g]]
                    nc.tensor.transpose(dst[:, 0:P], probs[:, g * P:(g + 1) * P], ident)
                    for k in range(NT):
                        last = nc.tensor.transpose(dst[:, (k + 1) * P:(k + 2) * P],
                                                   probs[:, 384 + g * S + k * P:384 + g * S + (k + 1) * P], ident)
                    last.then_inc(probs_t_done, 1)
                rows = slice(HEAD_DIM * (s % 2), HEAD_DIM * (s % 2 + 1))
                for g in range(NG):
                    pe.wait_ge(probs_t_read, NG * s + g + 1)
                    cols = slice((g * HEAD_SLOTS + s) * HEAD_DIM, (g * HEAD_SLOTS + s + 1) * HEAD_DIM)
                    c0 = (s // 2) * S
                    nc.tensor.matmul(bank[3][rows, c0:c0 + S], v_tok[:, 0, cols], probs_t[:, g, 0:S],
                                     start=g == 0, stop=False)
                    last = nc.tensor.matmul(bank[3][rows, c0 + P:c0 + S], v_tok[:, 1, cols], probs_t[:, g, S:S + P],
                                            start=False, stop=g == NG - 1)
                if s == HEAD_SLOTS - 1:
                    last.then_inc(attn_done, 1)
                if s >= 1:
                    row(6 + s)
                job(JOB_GATES + 2 * s + 1)

            pe.wait_ge(ld_pool, 32)
            pe.wait_ge(pooled, 1)
            for n in range(2):
                pe.wait_ge(job_read, JOB_POOL + n - 1)
                for q in range(2):
                    g = 2 * n + q
                    last = nc.tensor.matmul(job_bank(JOB_POOL + n)[:, q * S:(q + 1) * S], pool_w_sb[:, g, :],
                                            mixed[:, g, :], start=True, stop=True)
                last.then_inc(job_done, 1)
            row(10)
            row(11)

            pe.wait_ge(job_read, JOB_POOL + 2)
            pe.wait_ge(attn_t_ready, 1)
            wp, wa = unit_view(("pool_out", 0)), unit_view(("attn_out", 0))
            landed(pe, ("attn_out", 0))
            landed(pe, ("pool_out", 0))
            for n in range(KT // 2):
                if n >= 2:
                    pe.wait_ge(merged, n - 1)
                for w, src, kk, b in ((wp, xp_t, 4, 6), (wa, attn_t, 2, 0)):
                    for q in range(2):
                        f = 2 * n + q
                        for k in range(kk):
                            last = nc.tensor.matmul(bank[b + n % 2][:, q * S:(q + 1) * S],
                                                    w[:, k, f * P:(f + 1) * P], src[:, k, :],
                                                    start=k == 0, stop=k == kk - 1)
                last.then_inc(branch_done, 1)

            pe.wait_ge(row_ready, 8)
            pe.wait_ge(merged, KT // 2)
            for t in range(NT):
                for hf in range(2):
                    for k in range(KT):
                        u = ("o", k // 4)
                        if t == 0 and hf == 0 and k % 4 == 0:
                            landed(pe, u)
                        last = nc.tensor.matmul(bank[2 + 2 * t + hf][:, :], gates[:, k, t * P:(t + 1) * P],
                                                unit_view(u)[:, k % 4, hf * HALF:(hf + 1) * HALF],
                                                start=k == 0, stop=k == KT - 1)
                    last.then_inc(mix_done, 1)

            pe.wait_ge(ld_router, 32)
            for t in range(NT):
                pe.wait_ge(u2_ready, t + 1)
                for k in range(KT):
                    last = nc.tensor.transpose(bank[(6, 0)[t] + k // 4][:, (k % 4) * P:(k % 4 + 1) * P],
                                               u2[:, t, k * P:(k + 1) * P], ident)
                last.then_inc(u2_t_done, 1)
                pe.wait_ge(u2_t_ready, 2 * (t + 1))
                for k in range(KT):
                    nc.tensor.matmul(bank[2 + t][:, 0:NE], u_t[:, k, t * P:(t + 1) * P], router_w[:, k, :],
                                     start=k == 0, stop=False)
                nc.tensor.matmul(bank[2 + t][:, 0:NE], one[0:1, :].to_broadcast([1, P]), b_router_sb,
                                 start=False, stop=True).then_inc(logits_done, 1)

            pe.wait_ge(scaled_ready, 1)
            pe.wait_ge(top_ready, NT)
            for t in range(NT):
                for hf in range(2):
                    nc.tensor.matmul(bank[2 * t + hf][:, :], scaled_ident, x_tok[:, t, hf * HALF:(hf + 1) * HALF],
                                     start=True, stop=False)

            pe.wait_ge(weight_ready, 1)
            pe.wait_ge(tri_ready, 1)
            nc.tensor.matmul(Y_BANK[:, 0:NE], tri_bf, chosen[:, 0, :], start=True, stop=True)
            nc.tensor.matmul(Y_BANK[:, NE:2 * NE], one_bf[:, 0:1].to_broadcast([P, P]), chosen[:, 0, :],
                             start=True, stop=False)
            nc.tensor.matmul(Y_BANK[:, NE:2 * NE], tri_bf, chosen[:, 1, :], start=False, stop=True) \
              .then_inc(rank_done, 1)
            for t in range(NT):
                last = nc.tensor.transpose(M_BANK[0:NE, t * P:(t + 1) * P], weight[:, t, 0:NE], ident)
            last.then_inc(weight_t_done, 1)
            def gather(b):
                for k in range(KT):
                    for t in range(NT):
                        for m in range(3):
                            last = nc.tensor.matmul(M_BANK[:, k * CAP:(k + 1) * CAP],
                                                    u2_parts[:, m, t, k * P:(k + 1) * P], pick_tok[:, b, t, :],
                                                    start=(t, m) == (0, 0), stop=(t, m) == (NT - 1, 2))
                return last

            def transpose_scatter():
                for t in range(NT):
                    for hf in range(2):
                        start = 64 - 64 * hf
                        n = 2 * t + hf
                        last = nc.tensor.transpose(M_BANK[:, n * P:(n + 1) * P], scatter[:, t, start:start + P],
                                                   ident)
                return last

            def stream(dst, lhs, w, k0, first, last_one):
                for k in range(4):
                    for hf in range(2):
                        last = nc.tensor.matmul(dst[hf * CAP:(hf + 1) * CAP, :], lhs(k0 + k),
                                                w[:, k, hf * HALF:(hf + 1) * HALF],
                                                start=first and k == 0, stop=last_one and k == 3)
                return last

            def add_bias(dst, b, which):
                for hf in range(2):
                    last = nc.tensor.matmul(dst[hf * CAP:(hf + 1) * CAP, :], pick_bias[:, b, :],
                                            bias_parts[:, which, hf * HALF:(hf + 1) * HALF],
                                            start=False, stop=True)
                return last

            def hidden_t(kt):
                return h_t[:, kt % 4, (kt // 4) * CAP:(kt // 4 + 1) * CAP]

            def transpose_hidden():
                for k in range(4):
                    last = nc.tensor.transpose(M_BANK[:, k * P:(k + 1) * P], h[:, k * P:(k + 1) * P], ident)
                return last

            def combine(t, b, values, stop):
                for hf in range(2):
                    last = nc.tensor.matmul(bank[2 * t + hf][:, :], scatter_t[:, b, 2 * t + hf, :], values,
                                            start=False, stop=stop)
                return last

            pe.wait_ge(picked, 1)
            pe.wait_ge(part_ready, 3 * NT)
            pe.wait_ge(weight_t_ready, 1)
            gather(0).then_inc(gather_done, 1)
            pe.wait_ge(b_down_ready, 1)
            for t in range(NT):
                for hf in range(2):
                    cols = slice(hf * HALF, (hf + 1) * HALF)
                    last = nc.tensor.matmul(bank[2 * t + hf][:, :], weight_t[:, t * P:(t + 1) * P],
                                            b_down_sb[:, cols], start=False, stop=False)
            last.then_inc(seed_done, 1)
            with pe.Fori(0, TURNS) as i:
                for j in range(BODY):
                    n0 = UNITS * j
                    b = j % 2

                    def unit_landed(k):
                        s = RING[(n0 + k) % SLOTS]
                        fills = FILLS[s] + (n0 + k) // SLOTS + 1
                        pe.wait_ge(slot_landed[s], i * (16 * BODY * UNITS // SLOTS) + 16 * fills)

                    pe.wait_ge(picked, i * BODY + (j + 2))
                    pe.wait_ge(misc_read, i * (3 * BODY) + (3 * j + 1))
                    gather(1 - b).then_inc(gather_done, 1)
                    for k in range(2):
                        unit_landed(k)
                        stream(G_BANK, lambda kt: x_sel[:, b, kt, :], expert_view(n0 + k), 4 * k, k == 0, False) \
                            .then_inc(pe_unit_used, 1)
                    add_bias(G_BANK, b, 0).then_inc(gate_done, 1)
                    pe.wait_ge(scatter_ready, i * BODY + (j + 1))
                    pe.wait_ge(misc_read, i * (3 * BODY) + (3 * j + 2))
                    transpose_scatter().then_inc(scatter_t_done, 1)
                    for k in range(2):
                        unit_landed(2 + k)
                        stream(U_BANK, lambda kt: x_sel[:, b, kt, :], expert_view(n0 + 2 + k), 4 * k, k == 0, False) \
                            .then_inc(pe_unit_used, 1)
                    add_bias(U_BANK, b, 1).then_inc(up_done, 1)
                    pe.wait_ge(y_ready, i * BODY + (j + 1))
                    for t in range(NT):
                        combine(t, 1 - b, y, False)
                    pe.wait_ge(h_ready, i * BODY + (j + 1))
                    pe.wait_ge(misc_read, i * (3 * BODY) + (3 * j + 3))
                    transpose_hidden().then_inc(h_t_done, 1)
                    pe.wait_ge(misc_read, i * (3 * BODY) + (3 * j + 4))
                    for k in range(2):
                        unit_landed(4 + k)
                        stream(Y_BANK, hidden_t, expert_view(n0 + 4 + k), 4 * k, k == 0, k == 1) \
                            .then_inc(pe_unit_used, 1)
            pe.wait_ge(most_ready, 1)
            most = pe.value_load(most_i[0:1, :], min_val=0, max_val=S)
            with pe.If(most > CAP):
                pe.wait_ge(y_ready, NE + 1)
                pe.sem_inc(ovf_pe, 1)
                with pe.Fori(0, NE) as e:
                    pe.wait_ge(ovf_landed, e * (16 * UNITS) + 16 * UNITS)
                    for n in range(CHUNKS):
                        def act_step(k):
                            pe.wait_ge(ovf_act, e * (4 * CHUNKS) + (4 * n + k))

                        def dve_step(k):
                            pe.wait_ge(ovf_dve, e * (4 * CHUNKS) + (4 * n + k))

                        dve_step(1)
                        gather(0).then_inc(ovf_pe, 1)
                        act_step(1)
                        transpose_scatter().then_inc(ovf_pe, 1)
                        act_step(2)
                        for k in range(2):
                            stream(G_BANK, lambda kt: x_sel[:, 0, kt, :], expert_view(k), 4 * k, k == 0, False)
                        add_bias(G_BANK, 0, 0)
                        for k in range(2):
                            stream(U_BANK, lambda kt: x_sel[:, 0, kt, :], expert_view(2 + k), 4 * k, k == 0, False)
                        add_bias(U_BANK, 0, 1).then_inc(ovf_pe, 1)
                        dve_step(3)
                        transpose_hidden().then_inc(ovf_pe, 1)
                        act_step(4)
                        for k in range(2):
                            last = stream(Y_BANK, hidden_t, expert_view(4 + k), 4 * k, k == 0, k == 1)
                        last.then_inc(ovf_pe, 1)
                        dve_step(4)
                        for t in range(NT):
                            last = combine(t, 0, y_late, False)
                        last.then_inc(ovf_pe, 1)

            pe.wait_ge(y_ready, NE + 1)
            for t in range(NT):
                combine(t, (NE - 1) % 2, y, True).then_inc(combined, 1)


INPUTS = ["x", "c", "positions", "w_ada", "b_ada", "w_in", "pool_w", "pool_scale", "w_pool_out", "w_attn_out",
          "w_o", "ln1_g", "ln1_b", "w_router", "b_router", "w_gate", "b_gate", "w_up", "b_up", "w_down", "b_down",
          "ln2_g", "ln2_b"]


def kernel(**inputs):
    import concourse.bacc as bacc
    from concourse.bass_utils import run_bass_kernel_spmd

    nc = bacc.Bacc("TRN2", target_bir_lowering=False, num_devices=1)
    const_table, mask_table = constants()
    arrays = {name: np.ascontiguousarray(inputs[name]) for name in INPUTS}
    arrays["const_table"], arrays["mask_table"] = const_table, mask_table
    aps = [nc.dram_tensor(name, a.shape, mybir.dt.from_np(a.dtype), kind="ExternalInput").ap()
           for name, a in arrays.items()]
    out = nc.dram_tensor("out", (1, S, D), F32, kind="ExternalOutput").ap()
    layer_kernel(nc, *aps, out)
    r = run_bass_kernel_spmd(nc, [arrays], core_ids=[0])
    return r.results[0]["out"]
```

```python
import math
from contextlib import ExitStack

import numpy as np

import concourse.bass as bass
from concourse import mybir

F32 = mybir.dt.float32
BF16 = mybir.dt.bfloat16
I32 = mybir.dt.int32
U32 = mybir.dt.uint32
ALU = mybir.AluOpType
ACT = mybir.ActivationFunctionType
AX = mybir.AxisListType

P = 128
D = 1024
S = 256
NT = S // P
KT = D // P
HALF = 512
POOL_WIDTH = D // 2
POOL_WINDOWS = (2, 4, 8, 16)
PG = len(POOL_WINDOWS)
HEAD_DIM = 64
GROUPS = ((128, 1), (512, 4), (2048, 16))
NG = len(GROUPS)
HEAD_SLOTS = 4
ATTN_WIDTH = NG * HEAD_SLOTS * HEAD_DIM
QT = ATTN_WIDTH // P
ROT_DIM = HEAD_DIM // 4
ROPE_THETA = 500000.0
NE = 32
TOP_K = 4
CAP = 64
CHUNKS = S // CAP - 1
SWIGLU_ALPHA = 1.702
SWIGLU_LIMIT = 7.0
DN_ALPHA = 2.0 ** 0.25
LN_EPS = 1e-5
NEG_INF = -1e30

SLOT = 4096
SLOTS = 8
FRONT_SLOTS = 6
EXTRA = 2
UNITS = 6
BODY = 4
TURNS = NE // BODY
DVE_KT = 6

FRONT = [("ada", 0), ("ada", 1), ("ada", 2), ("ada", 3), ("in", 1), ("in", 2), ("in", 3), ("ada", 4),
         ("in", 4), ("ada", 5), ("in", 5), ("ada", 6), ("in", 0), ("ada", 7), ("in", 6), ("ada", 8),
         ("in", 7), ("ada", 9), ("in", 8), ("ada", 10), ("in", 9), ("ada", 11), ("attn_out", 0),
         ("pool_out", 0), ("o", 0), ("o", 1)]
IN_COLS = [(0, 512), (512, 1024), (1024, 1536), (1536, 2048), (2048, 2560), (2560, 2816)] + \
          [(2816 + 512 * j, 3328 + 512 * j) for j in range(4)]
SLOT_OF = {u: n % FRONT_SLOTS for n, u in enumerate(FRONT)}
TURN_OF = {u: n // FRONT_SLOTS + 1 for n, u in enumerate(FRONT)}
FILLS = [sum(n % FRONT_SLOTS == s for n in range(len(FRONT))) if s < FRONT_SLOTS else 0 for s in range(SLOTS)]
RING = [6, 7, 2, 3, 4, 5, 0, 1]

C_IDENT, C_PERM, C_TRI = 0, 128, 256
C_RANKS, C_EXPERTS, C_PICK, C_RCNT = 384, 448, 480, 512
C_FREQ, C_EPS, C_DROP1, C_DROP2, C_ONE = 576, 577, 578, 579, 580
N_CONST = 581
PADDED = NE + 2

TWO_PI_PARTS = []
_rest = 2.0 * math.pi
for _bits in (8, 8, 8, 24):
    _m, _e = math.frexp(_rest)
    TWO_PI_PARTS.append(math.ldexp(round(_m * 2 ** _bits), _e - _bits))
    _rest -= TWO_PI_PARTS[-1]
ROUND = 1.5 * 2.0 ** 23


def constants():
    c = np.zeros((P, N_CONST), np.float32)
    p = np.arange(P)
    c[:, C_IDENT:C_IDENT + P] = np.eye(P)
    for m in range(P):
        j = m % HEAD_DIM
        if j < ROT_DIM // 2:
            c[m + ROT_DIM // 2, C_PERM + m] = -1.0
        elif j < ROT_DIM:
            c[m - ROT_DIM // 2, C_PERM + m] = 1.0
    c[:, C_TRI:C_TRI + P] = p[:, None] < p[None, :]
    c[:, C_RANKS:C_RANKS + CAP] = np.arange(1, CAP + 1)
    c[:, C_EXPERTS:C_EXPERTS + NE] = np.arange(NE)
    c[:, C_PICK:C_PICK + NE] = (p % 32)[:, None] == np.arange(NE)[None]
    t = np.arange(16)
    for g, w in enumerate(POOL_WINDOWS):
        c[:, C_RCNT + 16 * g:C_RCNT + 16 * g + 16] = 1.0 / np.minimum(t + 1, w)
    j = p % HEAD_DIM
    freq = np.power(ROPE_THETA, -(j % (ROT_DIM // 2)) * (2.0 / ROT_DIM))
    c[:, C_FREQ] = np.where(j < ROT_DIM, freq, 0.0)
    c[:, C_EPS] = LN_EPS
    c[:, C_DROP1] = -(p >= 32).astype(np.float32)
    c[:, C_DROP2] = -(p >= 64).astype(np.float32)
    c[:, C_ONE] = 1.0
    q, k = np.arange(P)[:, None], np.arange(P)[None]
    masks = np.zeros((P, NG, 2, P), np.float32)
    for g, (window, dilation) in enumerate(GROUPS):
        for tile, dist in enumerate((P + q - k, q - k)):
            ok = (dist >= 0) & (dist <= window) & (dist % dilation == 0)
            masks[:, g, tile] = np.where(ok, 0.0, NEG_INF)
    return c, masks.reshape(P, NG * 2 * P)


def layer_kernel(nc, x, c, positions, w_ada, b_ada, w_in, pool_w, pool_scale, w_pool_out, w_attn_out, w_o,
                 ln1_g, ln1_b, w_router, b_router, w_gate, b_gate, w_up, b_up, w_down, b_down, ln2_g, ln2_b,
                 const_table, mask_table, out):
    ctx = ExitStack()
    with ctx:
        def sb(name, shape, dt=F32):
            return ctx.enter_context(nc.sbuf_tensor(name, shape, dt))

        def sem(name):
            return ctx.enter_context(nc.semaphore(name))

        ring = sb("ring", [P, SLOTS * SLOT])
        const = sb("const", [P, N_CONST])
        x_tok = sb("x_tok", [P, NT, D])
        ln_tok = sb("ln_tok", [P, NT * D])
        feat_region = sb("feat_region", [P, KT * S])
        pool_region = sb("pool_region", [P, 2048])
        gate_region = sb("gate_region", [P, 4096])
        attn_region = sb("attn_region", [P, 704])
        acc_region = sb("acc_region", [P, 1024])
        row_region = sb("row_region", [P, 4096])
        bias_parts = sb("bias_parts", [96, 2, D], BF16)
        ada_parts = sb("ada_parts", [96, HALF], BF16)
        router_w = sb("router_w", [P, KT + 1, NE])
        small = sb("small", [P, 104])

        def view(t, start, size, dt=F32, parts=P):
            a = t[0:parts, start:start + size]
            return a if dt is F32 else a.bitcast(dt)

        late = FRONT_SLOTS * SLOT
        qk = view(ring, late, 2 * QT * S).rearrange("p (j t) -> p j t", j=2 * QT)
        v_tok = view(ring, late + 3072, NT * ATTN_WIDTH).rearrange("p (t n) -> p t n", t=NT)
        probs = view(ring, late + 4608, 1152)
        probs_t = view(ring, late + 5760, 1152).rearrange("p (g n) -> p g n", g=NG)
        cos = view(ring, late + 6912, S)
        sin = view(ring, late + 7168, S)
        masks = view(ring, late + 7424, NG * 2 * P).rearrange("p (g k n) -> p g k n", g=NG, k=2)
        rot_tmp = view(ring, late + 4608, 2 * S).rearrange("p (j t) -> p j t", j=2)
        pos_i = view(ring, late + 5760, S, I32)
        angle = view(ring, late + 5760 + S, S)
        turns = view(ring, late + 5760 + 2 * S, S)

        xn = ln_tok[:, :].rearrange("p (t n) -> p t n", t=NT)
        u2 = xn
        u_t = feat_region[:, :].rearrange("p (k t) -> p k t", k=KT)
        xp_t = view(pool_region, 0, PG * S).rearrange("p (g t) -> p g t", g=PG)
        mixed = view(pool_region, 1024, PG * S).rearrange("p (g t) -> p g t", g=PG)
        ln_rows = pool_region[:, :].rearrange("p (r n) -> p r n", r=2)
        gates = gate_region[:, :].rearrange("p (j t) -> p j t", j=2 * KT)
        pool_tmp = gates[:, 12:16, :]
        bias_raw = view(gate_region, 0, 2 * D, parts=96).rearrange("p (m n) -> p m n", m=2)
        attn_t = view(attn_region, 0, 2 * S).rearrange("p (j t) -> p j t", j=2)
        ada_acc = acc_region[:, :].rearrange("p (b n) -> p b n", b=2)
        ada_rows = row_region[:, :].rearrange("p (r n) -> p r n", r=4)
        pool_w_sb = view(row_region, 3584, PG * P).rearrange("p (g d) -> p g d", g=PG)
        b_ada_raw = view(feat_region, 0, HALF, parts=96)

        c_col, c_silu, c_sig = small[:, 0:8], small[:, 8:16], small[:, 16:24]
        shift1, scale1 = small[:, 24:32], small[:, 32:40]
        stats = small[:, 40:64].rearrange("p (t h s) -> p t h s", t=NT, h=2)
        moments = small[:, 64:68].rearrange("p (t s) -> p t s", t=NT)
        std, rstd = small[:, 68:70], small[:, 70:72]
        row_max, row_sum, row_inv = small[:, 72:74], small[:, 74:76], small[:, 76:78]
        pool_scale_c = small[:, 78:82]
        most_f, most_all = small[:, 82:83], small[:, 83:84]
        most_i = small[:, 84:85].bitcast(I32)
        one_bf = small[:, 85:86].bitcast(BF16)
        pick_rows = small[:, 86:102].bitcast(BF16)

        top_v = view(attn_region, 64, 16).rearrange("p (t k) -> p t k", t=NT)
        top_i = view(attn_region, 80, 16, U32).rearrange("p (t k) -> p t k", t=NT)
        top_f = view(attn_region, 96, 16).rearrange("p (t k) -> p t k", t=NT)
        top_e = view(attn_region, 112, 8).rearrange("p (t k) -> p t k", t=NT)
        top_n, top_s, top_r = (view(attn_region, 120 + 2 * k, 2) for k in range(3))
        terms = view(attn_region, 128, NT * TOP_K * NE).rearrange("p (t k e) -> p t k e", t=NT, k=TOP_K)
        weight = view(attn_region, 384, NT * PADDED).rearrange("p (t e) -> p t e", t=NT)
        rank1 = view(attn_region, 452, NT * PADDED).rearrange("p (t e) -> p t e", t=NT)
        chosen = view(attn_region, 520, 32, BF16).rearrange("p (t e) -> p t e", t=NT)
        b_router_sb = router_w[0:1, KT, :]
        tri_bf = view(attn_region, 584, 64, BF16)
        chosen_f = terms[:, :, 0, :]

        u2_parts = view(gate_region, 0, 3072, BF16).rearrange("p (m t n) -> p m t n", m=3, t=NT)
        y = view(gate_region, 3072, HALF)
        gate_min = view(gate_region, 3584, HALF)
        x_sel = view(feat_region, 0, 1024).rearrange("p (b k r) -> p b k r", b=2, k=KT)
        h = view(feat_region, 1024, HALF)
        h_t = view(feat_region, 1536, HALF).rearrange("p (c n) -> p c n", c=4)
        sig = view(acc_region, 0, HALF)
        up_c = view(acc_region, 512, HALF)
        scatter_t = view(ln_tok, 0, 1024).rearrange("p (b m t) -> p b m t", b=2, m=4)
        scatter = view(row_region, 0, NT * 192).rearrange("p (t r) -> p t r", t=NT)
        pick_tok = view(row_region, 384, 128, BF16).rearrange("p (b t r) -> p b t r", b=2, t=NT)
        gate2_halves = view(row_region, 512, HALF)
        pick_bias = view(attn_region, 0, 64, BF16, parts=96).rearrange("p (b r) -> p b r", b=2)
        late_rank = view(attn_region, 648, 2).rearrange("p (t r) -> p t r", t=NT)
        scaled_ident = view(acc_region, 0, P)
        y_late = x_tok[:, 0, 0:HALF]

        ident = const[:, C_IDENT:C_IDENT + P]
        ranks = const[:, C_RANKS:C_RANKS + CAP]
        one = const[:, C_ONE:C_ONE + 1]
        eps = const[:, C_EPS:C_EPS + 1]

        bank = [ctx.enter_context(nc.psum_tensor(f"bank{b}", [P, HALF], F32)) for b in range(8)]
        T_BANKS = (4, 0, 1)
        G_BANK, U_BANK, Y_BANK, M_BANK = bank[4], bank[5], bank[6], bank[7]

        def slot(s):
            return ring[:, s * SLOT:(s + 1) * SLOT]

        def unit_view(u):
            s = slot(SLOT_OF[u])
            if u[0] in ("ada", "in"):
                n = HALF if u[0] == "ada" else IN_COLS[u[1]][1] - IN_COLS[u[1]][0]
                return s[:, 0:KT * n].rearrange("p (k n) -> p k n", k=KT)
            k = 2 if u[0] == "attn_out" else 4
            return s[:, 0:k * D].rearrange("p (k n) -> p k n", k=k)

        def unit_source(u):
            kind, j = u
            if kind == "ada":
                w = w_ada[0][:, HALF * j:HALF * (j + 1)]
            elif kind == "in":
                w = w_in[0][:, IN_COLS[j][0]:IN_COLS[j][1]]
            elif kind == "o":
                w = w_o[0][HALF * j:HALF * (j + 1), :]
            else:
                w = (w_attn_out if kind == "attn_out" else w_pool_out)[0]
            return w.rearrange("(k p) n -> p k n", p=P)

        expert_rows = [w[0].rearrange("e k n -> (e k) n") for w in (w_gate, w_up, w_down)]

        def expert_view(m):
            return slot(RING[m % SLOTS]).rearrange("p (k n) -> p k n", k=4)

        late_rows = row_region[:, D:4 * D].rearrange("p (k n) -> p k n", k=3)
        extra_tiles = [[ln_rows[:, 0, :], ln_rows[:, 1, :], x_tok[:, 0, :], x_tok[:, 1, :]],
                       [late_rows[:, 0, :], late_rows[:, 1, :], late_rows[:, 2, :], ln_tok[:, D:2 * D]]]

        def expert_source(expert, k):
            rows = expert_rows[k // 2][bass.ds(expert * D + HALF * (k % 2), HALF), :]
            return rows.rearrange("(k p) n -> p k n", p=P)

        ld_x, ld_c, ld_const, ld_masks = [sem("ld_x0"), sem("ld_x1")], sem("ld_c"), sem("ld_const"), sem("ld_masks")
        ld_b_ada, ld_pos, ld_pool, ld_bias = sem("ld_b_ada"), sem("ld_pos"), sem("ld_pool"), sem("ld_bias")
        ld_ln1, ld_router, ld_b_down, ld_ln2 = sem("ld_ln1"), sem("ld_router"), sem("ld_b_down"), sem("ld_ln2")
        slot_landed = [sem(f"slot{s}_landed") for s in range(SLOTS)]
        pe_unit_used = sem("pe_unit_used")
        raw_cleared = sem("raw_cleared")
        pick_ready = sem("pick_ready")
        sig_c_ready = sem("sig_c_ready")
        silu_ready = sem("silu_ready")
        dve_chain = sem("dve_chain")
        std_ready = sem("std_ready")
        moments_ready = sem("moments_ready")
        xn_ready = sem("xn_ready")
        xn_t_done = sem("xn_t_done")
        acc_ready = sem("acc_ready")
        acc_read = sem("acc_read")
        parts_ready = sem("parts_ready")
        ada_cols_ready = sem("ada_cols_ready")
        u_t_ready = sem("u_t_ready")
        row_ready = sem("row_ready")
        job_done = sem("job_done")
        job_read = sem("job_read")
        angle_ready = sem("angle_ready")
        trig_ready = sem("trig_ready")
        partner_done = sem("partner_done")
        rotated = sem("rotated")
        scores_done = sem("scores_done")
        scores_read = sem("scores_read")
        exp_ready = sem("exp_ready")
        probs_ready = sem("probs_ready")
        probs_t_done = sem("probs_t_done")
        probs_t_read = sem("probs_t_read")
        attn_done = sem("attn_done")
        attn_t_ready = sem("attn_t_ready")
        pool_chain = sem("pool_chain")
        pooled = sem("pooled")
        branch_done = sem("branch_done")
        merged = sem("merged")
        mix_done = sem("mix_done")
        u2_ready = sem("u2_ready")
        u2_t_done = sem("u2_t_done")
        u2_t_ready = sem("u2_t_ready")
        part_ready = sem("part_ready")
        rest_ready = sem("rest_ready")
        rest_dve_ready = sem("rest_dve_ready")
        logits_done = sem("logits_done")
        top_ready = sem("top_ready")
        top_exp_ready = sem("top_exp_ready")
        weight_ready = sem("weight_ready")
        weight_t_done = sem("weight_t_done")
        weight_t_ready = sem("weight_t_ready")
        rank_done = sem("rank_done")
        tri_ready = sem("tri_ready")
        moe_chain = sem("moe_chain")
        moe_cleared = sem("moe_cleared")
        scaled_ready = sem("scaled_ready")
        seeded = sem("seeded")
        extra_landed = [sem("extra0_landed"), sem("extra1_landed")]
        y_cleared = sem("y_cleared")
        scatter_t_cleared = sem("scatter_t_cleared")
        gate2_ready = sem("gate2_ready")
        most_f_ready = sem("most_f_ready")
        most_all_ready = sem("most_all_ready")
        most_ready = sem("most_ready")
        picked = sem("picked")
        scatter_ready = sem("scatter_ready")
        gather_done = sem("gather_done")
        scatter_t_done = sem("scatter_t_done")
        misc_read = sem("misc_read")
        gate_done, up_done = sem("gate_done"), sem("up_done")
        gate_min_ready = sem("gate_min_ready")
        sig_ready = sem("sig_ready")
        h_ready = sem("h_ready")
        h_t_done = sem("h_t_done")
        y_ready = sem("y_ready")
        combined = sem("combined")
        final_chain = sem("final_chain")
        final_moments = sem("final_moments")
        final_std = sem("final_std")
        out_ready = sem("out_ready")
        out_written = sem("out_written")
        ovf_landed = sem("ovf_landed")
        ovf_pe, ovf_act, ovf_dve = sem("ovf_pe"), sem("ovf_act"), sem("ovf_dve")
        ovf_chain = sem("ovf_chain")

        jobs = [(("in", 1 + n // 2), n % 2) for n in range(6)]
        jobs += [(("in", 4), 0), (("in", 4), 1), (("in", 5), 0)]
        jobs += [(("in", 0), 0), (("in", 0), 1)]
        JOB_GATES = len(jobs)
        jobs += [(("in", 6 + n // 2), n % 2) for n in range(8)]
        JOB_POOL = len(jobs)

        def job_bank(n):
            return bank[6 + n % 2]

        def landed(eng, u):
            eng.wait_ge(slot_landed[SLOT_OF[u]], 16 * TURN_OF[u])

        block = ctx.enter_context(nc.Block())

        @block.sync
        def _(sp):
            for t in range(NT):
                sp.dma_start(x_tok[:, t, :], x[0, t * P:(t + 1) * P, :]).then_inc(ld_x[t], 16)
            sp.wait_ge(raw_cleared, 1)
            for m in range(3):
                sp.dma_start(b_ada_raw[32 * m:32 * m + 12, :],
                             b_ada[0].rearrange("(j n) -> j n", j=12)).then_inc(ld_b_ada, 16)

            def wait_used(u):
                if u[0] == "ada" and u[1] < 4:
                    sp.wait_ge(acc_read, u[1] + 1)
                elif u[0] == "ada":
                    sp.wait_ge(acc_ready, u[1] + 1)
                elif u[0] == "in":
                    sp.wait_ge(job_done, max(n for n, (v, _) in enumerate(jobs) if v == u) + 1)
                elif u[0] == "o":
                    sp.wait_ge(mix_done, 2 * NT)
                else:
                    sp.wait_ge(branch_done, KT // 2)

            for n, u in enumerate(FRONT):
                if n >= FRONT_SLOTS:
                    wait_used(FRONT[n - FRONT_SLOTS])
                sp.dma_start(unit_view(u), unit_source(u)).then_inc(slot_landed[n % FRONT_SLOTS], 16)
            last_in_slot = {n % FRONT_SLOTS: u for n, u in enumerate(FRONT)}
            for m in range(SLOTS):
                if RING[m] < FRONT_SLOTS:
                    wait_used(last_in_slot[RING[m]])
                else:
                    sp.wait_ge(attn_done, 1)
                sp.dma_start(expert_view(m), expert_source(m // UNITS, m % UNITS)) \
                  .then_inc(slot_landed[RING[m]], 16)

            def source(m):
                return expert_source(m // UNITS, m % UNITS)

            sp.wait_ge(u2_ready, 2 * NT)
            sp.dma_start(ln_rows, source(SLOTS)[:, 0:2, :]).then_inc(extra_landed[0], 16)
            sp.wait_ge(gate2_ready, 1)
            sp.dma_start(late_rows, source(SLOTS + 1)[:, 0:3, :]).then_inc(extra_landed[1], 16)
            sp.wait_ge(part_ready, 3 * NT)
            sp.dma_start(ln_tok[:, D:2 * D], source(SLOTS + 1)[:, 3, :]).then_inc(extra_landed[1], 16)
            sp.wait_ge(seeded, 2 * NT)
            sp.dma_start(x_tok[:, :, :], source(SLOTS)[:, 2:4, :]).then_inc(extra_landed[0], 16)

            for m in range(SLOTS + EXTRA, BODY * UNITS):
                before = m - EXTRA - SLOTS
                if before == SLOTS:
                    sp.wait_ge(pe_unit_used, SLOTS + 1)
                    for r, w in enumerate((ln2_g, ln2_b)):
                        sp.dma_start(ln_rows[:, r, :], w.to_broadcast([P, D])).then_inc(ld_ln2, 16)
                sp.wait_ge(pe_unit_used, before + 1 if before < SLOTS else before + EXTRA + 1)
                sp.dma_start(expert_view(m - EXTRA), source(m)) \
                  .then_inc(slot_landed[RING[(m - EXTRA) % SLOTS]], 16)
            with sp.Fori(1, TURNS) as i:
                for n in range(BODY * UNITS):
                    sp.wait_ge(pe_unit_used, i * (BODY * UNITS) + (n - SLOTS + 1))
                    sp.dma_start(expert_view(n - EXTRA), expert_source(i * BODY + n // UNITS, n % UNITS)) \
                      .then_inc(slot_landed[RING[(n - EXTRA) % SLOTS]], 16)

            sp.wait_ge(most_ready, 1)
            most = sp.value_load(most_i[0:1, :], min_val=0, max_val=S)
            with sp.If(most > CAP):
                with sp.Fori(0, NE) as e:
                    sp.wait_ge(ovf_pe, e * (6 * CHUNKS) + 1)
                    for k in range(UNITS):
                        sp.dma_start(expert_view(k), expert_source(e, k)).then_inc(ovf_landed, 16)
            for t in range(NT):
                for hf in range(2):
                    cols = slice(hf * HALF, (hf + 1) * HALF)
                    sp.wait_ge(out_ready, 2 * t + hf + 1)
                    sp.dma_start(out[0, t * P:(t + 1) * P, cols], x_tok[:, t, cols]).then_inc(out_written, 16)
            sp.wait_ge(out_written, 16 * 2 * NT)

        @block.scalar
        def _(act):
            act.dma_start(c_col, c[0].rearrange("(k p) -> p k", p=P), allow_slow_non_contiguous=True).then_inc(ld_c, 16)
            act.dma_start(const[:, :], const_table).then_inc(ld_const, 16)
            act.wait_ge(ld_c, 16)
            nc.scalar.activation(c_sig, c_col, ACT.Sigmoid).then_inc(sig_c_ready, 1)
            act.wait_ge(ld_const, 16)
            nc.scalar.activation(one_bf, one.to_broadcast([P, 2]), ACT.Copy)
            nc.scalar.activation(pick_rows, const[:, C_PICK:C_PICK + NE], ACT.Copy).then_inc(pick_ready, 1)
            for t in range(NT):
                act.wait_ge(moments_ready, t + 1)
                nc.scalar.activation(std[:, t:t + 1], moments[:, t, 1:2], ACT.Sqrt, bias=eps).then_inc(std_ready, 1)

            act.dma_start(pos_i, positions.to_broadcast([P, S])).then_inc(ld_pos, 16)
            act.dma_start(masks, mask_table.rearrange("p (g k n) -> p g k n", g=NG, k=2)).then_inc(ld_masks, 16)
            for m in range(3):
                for j, b in enumerate((b_gate, b_up)):
                    act.dma_start(bias_raw[32 * m:32 * m + NE, j, :], b[0]).then_inc(ld_bias, 16)
            act.dma_start(pool_w_sb, pool_w[0].rearrange("g c d -> c g d")).then_inc(ld_pool, 16)
            act.dma_start(pool_scale_c, pool_scale[0].rearrange("(g d) -> d g", g=PG),
                          allow_slow_non_contiguous=True).then_inc(ld_pool, 16)
            act.dma_start(router_w[:, 0:KT, :], w_router[0].rearrange("(k p) e -> p k e", p=P)) \
               .then_inc(ld_router, 16)
            act.dma_start(b_router_sb, b_router).then_inc(ld_router, 16)

            act.wait_ge(ada_cols_ready, 1)
            act.wait_ge(xn_t_done, 1)
            for k in range(KT):
                nc.scalar.activation(u_t[:, k, :], bank[k // 2][:, (k % 2) * S:(k % 2 + 1) * S], ACT.Identity,
                                     bias=shift1[:, k:k + 1], scale=scale1[:, k:k + 1]).then_inc(u_t_ready, 1)

            def row(j, src=bank[5]):
                act.wait_ge(acc_read, j + 1)
                r = j - 4
                nc.scalar.activation(ada_rows[:, r // 2, (r % 2) * HALF:(r % 2 + 1) * HALF], src[:, :],
                                     ACT.Copy, bias=0.0 if r // 2 == 1 else 1.0).then_inc(row_ready, 1)

            def job(n):
                act.wait_ge(job_done, n + 1)
                src = job_bank(n)[:, :]
                pair = src.rearrange("p (j t) -> p j t", j=2)
                if n < 6:
                    nc.scalar.activation(qk[:, 2 * n:2 * n + 2, :], pair, ACT.Copy).then_inc(job_read, 1)
                elif n < 8:
                    nc.scalar.activation(v_tok[:, n - 6, 0:HALF], src, ACT.Copy).then_inc(job_read, 1)
                elif n == 8:
                    nc.scalar.activation(v_tok[:, :, HALF:ATTN_WIDTH], pair, ACT.Copy).then_inc(job_read, 1)
                elif n < JOB_GATES:
                    j = 2 * (n - 9)
                    nc.scalar.activation(xp_t[:, j:j + 2, :], pair, ACT.Copy).then_inc(job_read, 1)
                elif n < JOB_POOL:
                    j = 2 * (n - JOB_GATES)
                    if j == 0:
                        act.wait_ge(parts_ready, 3)
                    if j == 12:
                        act.wait_ge(pooled, 1)
                    nc.scalar.activation(gates[:, j:j + 2, :], pair, ACT.Sigmoid).then_inc(job_read, 1)
                else:
                    for j in range(2):
                        g = 2 * (n - JOB_POOL) + j
                        last = nc.scalar.activation(xp_t[:, g, :], pair[:, j, :], ACT.Copy,
                                                    scale=pool_scale_c[:, g:g + 1])
                    last.then_inc(job_read, 1)

            for n in range(2):
                job(n)
            for k, table in enumerate((sin, cos)):
                act.wait_ge(angle_ready, k + 1)
                nc.scalar.activation(table, rot_tmp[:, k, :], ACT.Sin).then_inc(trig_ready, 1)
            for n in range(2, 7):
                job(n)
            row(4)
            for n in (7, 8):
                job(n)
            row(5)
            for n in (9, 10):
                job(n)
            row(6)
            for s in range(HEAD_SLOTS):
                for t in range(NT):
                    act.wait_ge(scores_read, 2 * s + t + 1)
                    part = probs[:, 384 * t:384 * t + 384 * (t + 1)]
                    nc.scalar.activation(part, part, ACT.Exp, bias=row_max[:, t:t + 1],
                                         accum_out=row_sum[:, t:t + 1]).then_inc(exp_ready, 1)
                job(JOB_GATES + 2 * s)
                for g in range(NG):
                    act.wait_ge(probs_t_done, NG * s + g + 1)
                    nc.scalar.activation(probs_t[:, g, :], bank[T_BANKS[g]][:, 0:384], ACT.Copy) \
                      .then_inc(probs_t_read, 1)
                if s >= 1:
                    row(6 + s)
                job(JOB_GATES + 2 * s + 1)
            act.wait_ge(attn_done, 1)
            nc.scalar.activation(attn_t, bank[3][:, :].rearrange("p (j t) -> p j t", j=2), ACT.Copy) \
              .then_inc(attn_t_ready, 1)
            act.wait_ge(ld_pool, 32)
            for n in range(2):
                job(JOB_POOL + n)
            act.wait_ge(pooled, 1)
            act.wait_ge(merged, KT // 2)
            for r, w in enumerate((ln1_g, ln1_b)):
                act.dma_start(ln_rows[:, r, :], w.to_broadcast([P, D])).then_inc(ld_ln1, 16)
            act.wait_ge(y_cleared, 1)
            for hf in range(2):
                act.dma_start(y[hf * CAP:hf * CAP + NE, :], b_down[0][:, hf * HALF:(hf + 1) * HALF]) \
                   .then_inc(ld_b_down, 16)

            def norm_std(t, k):
                act.wait_ge(moments_ready, 2 + 2 * t + k + 1)
                nc.scalar.activation(std[:, t:t + 1], moments[:, t, 1:2], ACT.Sqrt, bias=eps).then_inc(std_ready, 1)

            def u2_t_half(t, b):
                act.wait_ge(u2_t_done, 2 * t + b + 1)
                nc.scalar.activation(u_t[:, 4 * b:4 * b + 4, t * P:(t + 1) * P],
                                     bank[6 + b][:, :].rearrange("p (k t) -> p k t", k=4),
                                     ACT.Copy).then_inc(u2_t_ready, 1)

            def part(t, m):
                if (t, m) == (1, 1):
                    act.wait_ge(rest_dve_ready, 1)
                elif m > 0:
                    act.wait_ge(rest_ready, (1, 2, 0, 3)[2 * t + m - 1])
                nc.scalar.activation(u2_parts[:, m, t, :], u2[:, t, :], ACT.Copy).then_inc(part_ready, 1)

            def top_exp(t):
                act.wait_ge(top_ready, t + 1)
                nc.scalar.activation(top_e[:, t, :], top_v[:, t, 0:TOP_K], ACT.Exp, bias=top_n[:, t:t + 1],
                                     accum_out=top_s[:, t:t + 1]).then_inc(top_exp_ready, 1)

            norm_std(0, 0)
            norm_std(0, 1)
            norm_std(1, 0)
            act.wait_ge(mix_done, 2 * NT)
            for b in range(2):
                u2_t_half(0, b)
            part(0, 0)
            row(10, bank[2])
            row(11, bank[3])
            nc.scalar.activation(scaled_ident, ident, ACT.Copy, scale=DN_ALPHA).then_inc(scaled_ready, 1)
            act.wait_ge(row_ready, 8)
            for hf in range(2):
                last = nc.scalar.activation(gate2_halves[hf * CAP:(hf + 1) * CAP, :],
                                            ada_rows[hf * CAP:(hf + 1) * CAP, 3, hf * HALF:(hf + 1) * HALF], ACT.Copy)
            last.then_inc(gate2_ready, 1)
            norm_std(1, 1)
            nc.scalar.activation(tri_bf, const[:, C_TRI:C_TRI + P], ACT.Copy).then_inc(tri_ready, 1)
            nc.scalar.activation(small[:, 102:103], eps, ACT.Exp)
            part(0, 1)
            act.wait_ge(u2_ready, 2 * NT)
            part(1, 0)
            top_exp(0)
            for b in range(2):
                u2_t_half(1, b)
            part(1, 1)
            top_exp(1)
            part(0, 2)
            part(1, 2)

            act.wait_ge(weight_t_done, 1)
            act.wait_ge(scatter_t_cleared, 1)
            for hf in range(2):
                rows = slice(hf * CAP, hf * CAP + NE)
                last = nc.scalar.activation(scatter_t[rows, 1, hf:4:2, :],
                                            U_BANK[rows, 0:S].rearrange("p (t n) -> p t n", t=NT), ACT.Copy)
            last.then_inc(weight_t_ready, 1)
            act.wait_ge(gather_done, 1)
            nc.scalar.activation(x_sel[:, 0], M_BANK[:, :].rearrange("p (k r) -> p k r", k=KT), ACT.Copy) \
              .then_inc(misc_read, 1)
            with act.Fori(0, TURNS) as i:
                for j in range(BODY):
                    act.wait_ge(gather_done, i * BODY + (j + 2))
                    nc.scalar.activation(x_sel[:, (j + 1) % 2], M_BANK[:, :].rearrange("p (k r) -> p k r", k=KT),
                                         ACT.Copy).then_inc(misc_read, 1)
                    act.wait_ge(scatter_t_done, i * BODY + (j + 1))
                    nc.scalar.activation(scatter_t[:, j % 2], M_BANK[:, :].rearrange("p (m t) -> p m t", m=4),
                                         ACT.Copy).then_inc(misc_read, 1)
                    act.wait_ge(gate_min_ready, i * BODY + (j + 1))
                    nc.scalar.activation(sig, gate_min, ACT.Sigmoid, scale=SWIGLU_ALPHA).then_inc(sig_ready, 1)
                    act.wait_ge(h_t_done, i * BODY + (j + 1))
                    nc.scalar.activation(h_t, M_BANK[:, :].rearrange("p (c n) -> p c n", c=4), ACT.Copy) \
                      .then_inc(misc_read, 1)

            act.wait_ge(most_ready, 1)
            most = act.value_load(most_i[0:1, :], min_val=0, max_val=S)
            with act.If(most > CAP):
                with act.Fori(0, NE) as e:
                    for n in range(CHUNKS):
                        act.wait_ge(ovf_pe, e * (6 * CHUNKS) + (6 * n + 2))
                        nc.scalar.activation(x_sel[:, 0], M_BANK[:, :].rearrange("p (k r) -> p k r", k=KT),
                                             ACT.Copy).then_inc(ovf_act, 1)
                        act.wait_ge(ovf_pe, e * (6 * CHUNKS) + (6 * n + 3))
                        nc.scalar.activation(scatter_t[:, 0], M_BANK[:, :].rearrange("p (m t) -> p m t", m=4),
                                             ACT.Copy).then_inc(ovf_act, 1)
                        act.wait_ge(ovf_dve, e * (4 * CHUNKS) + (4 * n + 2))
                        nc.scalar.activation(sig, gate_min, ACT.Sigmoid, scale=SWIGLU_ALPHA).then_inc(ovf_act, 1)
                        act.wait_ge(ovf_pe, e * (6 * CHUNKS) + (6 * n + 5))
                        nc.scalar.activation(h_t, M_BANK[:, :].rearrange("p (c n) -> p c n", c=4), ACT.Copy) \
                          .then_inc(ovf_act, 1)
            for t in range(NT):
                act.wait_ge(final_moments, t + 1)
                nc.scalar.activation(std[:, t:t + 1], moments[:, t, 1:2], ACT.Sqrt, bias=eps).then_inc(final_std, 1)

        @block.vector
        def _(dve):
            counts = {}

            def step(ins, s=dve_chain):
                counts[s.name] = counts.get(s.name, 0) + 1
                ins.then_inc(s, 1)
                dve.wait_ge(s, counts[s.name])

            def split(raw, parts):
                step(nc.vector.tensor_copy(parts, raw))
                for drop in (C_DROP1, C_DROP2):
                    step(nc.vector.scalar_tensor_tensor(out=raw, in0=parts, scalar=const[0:96, drop:drop + 1],
                                                        in1=raw, op0=ALU.mult, op1=ALU.add))
                    step(nc.vector.tensor_copy(parts, raw), parts_ready if drop == C_DROP2 else dve_chain)

            dve.wait_ge(sig_c_ready, 1)
            step(nc.vector.tensor_tensor(c_silu, c_col, c_sig, ALU.mult), silu_ready)

            def norm(src, dst, t, n_std):
                for hf in range(2):
                    step(nc.vector.bn_stats(stats[:, t, hf, :], src[:, t, hf * HALF:(hf + 1) * HALF]))
                step(nc.vector.bn_aggr(moments[:, t, :], stats[:, t]), moments_ready)
                dve.wait_ge(std_ready, n_std)
                step(nc.vector.reciprocal(rstd[:, t:t + 1], std[:, t:t + 1]))
                return nc.vector.tensor_scalar(dst[:, t, :], src[:, t, :], moments[:, t, 0:1], rstd[:, t:t + 1],
                                               ALU.subtract, ALU.mult)

            def scaled_norm(src, dst, t, n_std, scale_row, shift_row, s=dve_chain):
                step(nc.vector.bn_aggr(moments[:, t, :], stats[:, t]), moments_ready)
                step(nc.vector.scalar_tensor_tensor(out=dst[:, t, :], in0=src[:, t, :], scalar=moments[:, t, 0:1],
                                                    in1=scale_row, op0=ALU.subtract, op1=ALU.mult))
                dve.wait_ge(std_ready, n_std)
                step(nc.vector.reciprocal(rstd[:, t:t + 1], std[:, t:t + 1]))
                for hf in range(2):
                    cols = slice(hf * HALF, (hf + 1) * HALF)
                    step(nc.vector.scalar_tensor_tensor(out=dst[:, t, cols], in0=dst[:, t, cols],
                                                        scalar=rstd[:, t:t + 1], in1=shift_row[:, cols],
                                                        op0=ALU.mult, op1=ALU.add), s)
                    if s is dve_chain:
                        step(nc.vector.bn_stats(stats[:, t, hf, :], dst[:, t, cols]))

            for t in range(NT):
                dve.wait_ge(ld_x[t], 16)
                norm(x_tok, xn, t, t + 1).then_inc(xn_ready, 1)

            def ada(j):
                if j >= 2:
                    dve.wait_ge(acc_read, j - 1)
                landed(dve, ("ada", j))
                w, acc = unit_view(("ada", j)), ada_acc[:, j % 2, :]
                step(nc.vector.tensor_scalar(acc, w[:, 0, :], c_silu[:, 0:1], None, ALU.mult))
                tiles = DVE_KT if j < 4 else KT
                for k in range(1, tiles):
                    ins = nc.vector.scalar_tensor_tensor(out=acc, in0=w[:, k, :], scalar=c_silu[:, k:k + 1],
                                                         in1=acc, op0=ALU.mult, op1=ALU.add)
                    if k < tiles - 1:
                        step(ins)
                ins.then_inc(acc_ready, 1)

            dve.wait_ge(ld_const, 16)
            dve.wait_ge(ld_b_ada, 48)
            split(b_ada_raw, ada_parts[:, :])
            for j in range(4):
                ada(j)
            dve.wait_ge(acc_read, 4)
            for q in range(4):
                nc.vector.tensor_copy(shift1[:, q:8:4], bank[4 + q][:, 0:2])
                last = nc.vector.tensor_scalar(scale1[:, q:8:4], bank[4 + q][:, 2:4], 1.0, None, ALU.add)
            last.then_inc(ada_cols_ready, 1)

            dve.wait_ge(ld_pos, 16)
            step(nc.vector.tensor_copy(angle, pos_i))
            step(nc.vector.tensor_scalar(angle, angle, const[:, C_FREQ:C_FREQ + 1], None, ALU.mult))
            for k in range(2):
                r = rot_tmp[:, k, :]
                step(nc.vector.tensor_scalar(turns, angle, 1.0 / (2.0 * math.pi), 0.25 * k, ALU.mult, ALU.add))
                step(nc.vector.tensor_scalar(turns, turns, ROUND, None, ALU.add))
                step(nc.vector.tensor_scalar(turns, turns, -ROUND, None, ALU.add))
                src = angle
                for part in TWO_PI_PARTS:
                    step(nc.vector.scalar_tensor_tensor(out=r, in0=turns, scalar=-part, in1=src,
                                                        op0=ALU.mult, op1=ALU.add))
                    src = r
                step(nc.vector.tensor_scalar(r, r, 0.5 * math.pi * k, None, ALU.add))
                step(nc.vector.tensor_scalar(r, r, 3.1415925, -3.1415925, ALU.min, ALU.max), angle_ready)

            def rotate(n):
                dve.wait_ge(trig_ready, 2)
                dve.wait_ge(partner_done, n + 1)
                pair, part = qk[:, 2 * n:2 * n + 2, :], bank[2 + n % 2][:, :].rearrange("p (j t) -> p j t", j=2)
                cos2, sin2 = (a.unsqueeze(1).to_broadcast([P, 2, S]) for a in (cos, sin))
                step(nc.vector.tensor_tensor(rot_tmp, part, sin2, ALU.mult))
                step(nc.vector.tensor_tensor(pair, pair, cos2, ALU.mult))
                step(nc.vector.tensor_tensor(pair, pair, rot_tmp, ALU.add), rotated)

            for n in range(2):
                rotate(n)
            ada(4)
            for n in (2, 3):
                rotate(n)
            ada(5)
            for n in (4, 5):
                rotate(n)
            dve.wait_ge(ld_bias, 96)
            split(bias_raw[:, 0, :], bias_parts[:, 0, :])
            ada(6)
            split(bias_raw[:, 1, :], bias_parts[:, 1, :])
            ada(7)

            dve.wait_ge(ld_masks, 16)
            for s in range(HEAD_SLOTS):
                for t in range(NT):
                    dve.wait_ge(scores_done, 2 * s + t + 1)
                    if t == 0:
                        part = probs[:, 0:384]
                        step(nc.vector.scalar_tensor_tensor(
                            out=part.rearrange("p (g n) -> p g n", g=NG),
                            in0=bank[0][:, 0:384].rearrange("p (g n) -> p g n", g=NG), scalar=HEAD_DIM ** -0.5,
                            in1=masks[:, :, 1, :], op0=ALU.mult, op1=ALU.add))
                    else:
                        part = probs[:, 384:1152]
                        flat = masks.rearrange("p g k n -> p (g k n)")
                        step(nc.vector.scalar_tensor_tensor(
                            out=part[:, 0:512], in0=bank[1][:, :], scalar=HEAD_DIM ** -0.5,
                            in1=flat[:, 0:512], op0=ALU.mult, op1=ALU.add))
                        step(nc.vector.scalar_tensor_tensor(
                            out=part[:, 512:768], in0=bank[2][:, 0:256], scalar=HEAD_DIM ** -0.5,
                            in1=flat[:, 512:768], op0=ALU.mult, op1=ALU.add))
                    step(nc.vector.tensor_reduce(row_max[:, t:t + 1], part, AX.X, ALU.max, negate=True),
                         scores_read)
                for t in range(NT):
                    part = probs[:, 384 * t:384 * t + 384 * (t + 1)]
                    dve.wait_ge(exp_ready, 2 * s + t + 1)
                    step(nc.vector.reciprocal(row_inv[:, t:t + 1], row_sum[:, t:t + 1]))
                    step(nc.vector.tensor_scalar(part, part, row_inv[:, t:t + 1], None, ALU.mult), probs_ready)
                ada(8 + s)

            for n in range(KT // 2):
                dve.wait_ge(job_read, JOB_POOL + 2)
                dve.wait_ge(branch_done, n + 1)
                gp, ga = gates[:, 2 * n:2 * n + 2, :], gates[:, KT + 2 * n:KT + 2 * n + 2, :]
                bp, ba = (bank[b + n % 2][:, :].rearrange("p (j t) -> p j t", j=2) for b in (6, 0))
                step(nc.vector.tensor_tensor(gp, gp, bp, ALU.mult))
                step(nc.vector.tensor_tensor(ga, ga, ba, ALU.mult))
                step(nc.vector.tensor_tensor(gp, gp, ga, ALU.add), merged)

            step(nc.vector.memset(weight[:, :, NE:PADDED], 0.0), moe_chain)
            step(nc.vector.memset(rank1[:, :, NE:PADDED], 0.0), moe_chain)
            dve.wait_ge(row_ready, 6)
            for t in range(NT):
                for hf in range(2):
                    cols = slice(hf * HALF, (hf + 1) * HALF)
                    dve.wait_ge(mix_done, 2 * t + hf + 1)
                    step(nc.vector.tensor_tensor(xn[:, t, cols], bank[2 + 2 * t + hf][:, :], ada_rows[:, 0, cols],
                                                 ALU.mult))
                    step(nc.vector.scalar_tensor_tensor(out=x_tok[:, t, cols], in0=x_tok[:, t, cols],
                                                        scalar=DN_ALPHA, in1=xn[:, t, cols],
                                                        op0=ALU.mult, op1=ALU.add))
                    step(nc.vector.bn_stats(stats[:, t, hf, :], x_tok[:, t, cols]))
                dve.wait_ge(ld_ln1, 32)
                scaled_norm(x_tok, x_tok, t, 2 + 2 * t + 1, ln_rows[:, 0, :], ln_rows[:, 1, :])
                scaled_norm(x_tok, u2, t, 2 + 2 * t + 2, ada_rows[:, 2, :], ada_rows[:, 1, :], u2_ready)

            for t in range(NT):
                dve.wait_ge(logits_done, t + 1)
                logits = bank[4 + t][:, 0:NE]
                step(nc.vector.max(top_v[:, t, :], logits), moe_chain)
                step(nc.vector.tensor_scalar(top_n[:, t:t + 1], top_v[:, t, 0:1], -1.0, None, ALU.mult), top_ready)
                step(nc.vector.max_index(top_i[:, t, :], top_v[:, t, :], logits), moe_chain)
                step(nc.vector.tensor_copy(top_f[:, t, :], top_i[:, t, :]), moe_chain)
                dve.wait_ge(top_exp_ready, t + 1)
                step(nc.vector.reciprocal(top_r[:, t:t + 1], top_s[:, t:t + 1]), moe_chain)
                step(nc.vector.tensor_scalar(top_e[:, t, :], top_e[:, t, :], top_r[:, t:t + 1], None, ALU.mult),
                     moe_chain)
                for k in range(TOP_K):
                    ins = nc.vector.tensor_scalar(terms[:, t, k, :], const[:, C_EXPERTS:C_EXPERTS + NE],
                                                  top_f[:, t, k:k + 1], top_e[:, t, k:k + 1],
                                                  ALU.is_equal, ALU.mult)
                step(ins, moe_chain)
                step(nc.vector.tensor_reduce(weight[:, t, 0:NE], terms[:, t].rearrange("p k e -> p e k"),
                                             AX.X, ALU.add), moe_chain)
                if t == 0:
                    dve.wait_ge(part_ready, 3)
                    dve.wait_ge(u2_t_done, 2 * NT)
                    nc.vector.tensor_tensor(u2[:, 1, :], u2[:, 1, :], u2_parts[:, 0, 1, :], ALU.subtract) \
                      .then_inc(rest_dve_ready, 1)
            step(nc.vector.tensor_scalar(chosen, weight[:, :, 0:NE], 0.0, None, ALU.is_gt), weight_ready)
            step(nc.vector.tensor_scalar(chosen_f, weight[:, :, 0:NE], 0.0, None, ALU.is_gt), moe_chain)
            dve.wait_ge(rank_done, 1)
            step(nc.vector.scalar_tensor_tensor(out=rank1[:, :, 0:NE],
                                                in0=Y_BANK[:, 0:NT * NE].rearrange("p (t e) -> p t e", t=NT),
                                                scalar=1.0, in1=chosen_f, op0=ALU.add, op1=ALU.mult), moe_chain)

            def pick_expert(e, b):
                col = rank1[:, :, bass.ds(e, 1)].to_broadcast([P, NT, CAP])
                return nc.vector.tensor_tensor(pick_tok[:, b], ranks.unsqueeze(1).to_broadcast([P, NT, CAP]),
                                               col, ALU.is_equal)

            def pick_biases(e, b):
                col = const[0:96, C_PICK:C_PICK + NE + 1][:, bass.ds(e, 1)].to_broadcast([96, CAP])
                return nc.vector.tensor_scalar(pick_bias[:, b, :], col, 1.0, None, ALU.mult)

            dve.wait_ge(moe_cleared, 1)
            pick_biases(0, 0)
            pick_expert(0, 0).then_inc(picked, 1)
            pick_expert(1, 1).then_inc(picked, 1)
            step(nc.vector.tensor_tensor(scatter[:, :, 64:128], ranks.unsqueeze(1).to_broadcast([P, NT, CAP]),
                                         rank1[:, :, 0:1].to_broadcast([P, NT, CAP]), ALU.is_equal), moe_chain)
            nc.vector.tensor_tensor(scatter[:, :, 64:128], scatter[:, :, 64:128],
                                    weight[:, :, 0:1].to_broadcast([P, NT, CAP]), ALU.mult).then_inc(scatter_ready, 1)
            step(nc.vector.tensor_reduce(most_f, rank1[:, :, 0:NE], AX.XY, ALU.max), most_f_ready)

            dve.wait_ge(gate2_ready, 1)
            base = counts[moe_chain.name]
            own = 3
            with dve.Fori(0, TURNS) as i:
                for j in range(BODY):
                    def chain(ins, k):
                        ins.then_inc(moe_chain, 1)
                        dve.wait_ge(moe_chain, i * (BODY * own) + (base + j * own + k + 1))

                    dve.wait_ge(gate_done, i * BODY + (j + 1))
                    nc.vector.tensor_scalar(gate_min, G_BANK[:, :], SWIGLU_LIMIT, None, ALU.min) \
                      .then_inc(gate_min_ready, 1)
                    pick_biases(i * BODY + (j + 1), (j + 1) % 2)
                    pick_expert(i * BODY + (j + 2), j % 2).then_inc(picked, 1)
                    dve.wait_ge(scatter_t_done, i * BODY + (j + 1))
                    chain(nc.vector.tensor_tensor(
                        scatter[:, :, 64:128], ranks.unsqueeze(1).to_broadcast([P, NT, CAP]),
                        rank1[:, :, bass.ds(i * BODY + (j + 1), 1)].to_broadcast([P, NT, CAP]), ALU.is_equal), 0)
                    nc.vector.tensor_tensor(
                        scatter[:, :, 64:128], scatter[:, :, 64:128],
                        weight[:, :, bass.ds(i * BODY + (j + 1), 1)].to_broadcast([P, NT, CAP]), ALU.mult) \
                      .then_inc(scatter_ready, 1)
                    dve.wait_ge(up_done, i * BODY + (j + 1))
                    chain(nc.vector.tensor_scalar(up_c, U_BANK[:, :], SWIGLU_LIMIT, -SWIGLU_LIMIT,
                                                  ALU.min, ALU.max), 1)
                    dve.wait_ge(gate_min_ready, i * BODY + (j + 1))
                    chain(nc.vector.scalar_tensor_tensor(out=up_c, in0=up_c, scalar=1.0, in1=gate_min,
                                                         op0=ALU.add, op1=ALU.mult), 2)
                    dve.wait_ge(sig_ready, i * BODY + (j + 1))
                    nc.vector.tensor_tensor(h, up_c, sig, ALU.mult).then_inc(h_ready, 1)
                    dve.wait_ge(pe_unit_used, i * (BODY * UNITS) + UNITS * (j + 1))
                    nc.vector.tensor_tensor(y, Y_BANK[:, :], gate2_halves, ALU.mult).then_inc(y_ready, 1)

            dve.wait_ge(most_ready, 1)
            most = dve.value_load(most_i[0:1, :], min_val=0, max_val=S)
            own_ovf = 6
            with dve.If(most > CAP):
                with dve.Fori(0, NE) as e:
                    for n in range(CHUNKS):
                        k = [0]

                        def chain(ins):
                            k[0] += 1
                            ins.then_inc(ovf_chain, 1)
                            dve.wait_ge(ovf_chain, e * (CHUNKS * own_ovf) + (n * own_ovf + k[0]))

                        chain(nc.vector.tensor_scalar(late_rank, rank1[:, :, bass.ds(e, 1)], -float(CAP * (n + 1)),
                                                      None, ALU.add))
                        chain(pick_biases(e, 0))
                        chain(nc.vector.tensor_tensor(pick_tok[:, 0], ranks.unsqueeze(1).to_broadcast([P, NT, CAP]),
                                                      late_rank.to_broadcast([P, NT, CAP]), ALU.is_equal))
                        chain(nc.vector.tensor_copy(scatter[:, :, 64:128], pick_tok[:, 0]))
                        nc.vector.tensor_tensor(scatter[:, :, 64:128], scatter[:, :, 64:128],
                                                weight[:, :, bass.ds(e, 1)].to_broadcast([P, NT, CAP]),
                                                ALU.mult).then_inc(ovf_dve, 1)
                        dve.wait_ge(ovf_pe, e * (6 * CHUNKS) + (6 * n + 4))
                        nc.vector.tensor_scalar(gate_min, G_BANK[:, :], SWIGLU_LIMIT, None, ALU.min) \
                          .then_inc(ovf_dve, 1)
                        chain(nc.vector.tensor_scalar(up_c, U_BANK[:, :], SWIGLU_LIMIT, -SWIGLU_LIMIT,
                                                      ALU.min, ALU.max))
                        dve.wait_ge(ovf_dve, e * (4 * CHUNKS) + (4 * n + 2))
                        chain(nc.vector.scalar_tensor_tensor(out=up_c, in0=up_c, scalar=1.0, in1=gate_min,
                                                             op0=ALU.add, op1=ALU.mult))
                        dve.wait_ge(ovf_act, e * (4 * CHUNKS) + (4 * n + 3))
                        nc.vector.tensor_tensor(h, up_c, sig, ALU.mult).then_inc(ovf_dve, 1)
                        dve.wait_ge(ovf_pe, e * (6 * CHUNKS) + (6 * n + 6))
                        nc.vector.tensor_tensor(y_late, Y_BANK[:, :], gate2_halves, ALU.mult).then_inc(ovf_dve, 1)
                        assert k[0] == own_ovf

            n_final = [0]

            def final(ins):
                n_final[0] += 1
                ins.then_inc(final_chain, 1)
                dve.wait_ge(final_chain, n_final[0])

            dve.wait_ge(ld_ln2, 32)
            for t in range(NT):
                for hf in range(2):
                    dve.wait_ge(combined, 2 * t + hf + 1)
                    final(nc.vector.bn_stats(stats[:, t, hf, :], bank[2 * t + hf][:, :]))
                nc.vector.bn_aggr(moments[:, t, :], stats[:, t]).then_inc(final_moments, 1)
                dve.wait_ge(final_moments, t + 1)
                for hf in range(2):
                    cols = slice(hf * HALF, (hf + 1) * HALF)
                    final(nc.vector.scalar_tensor_tensor(out=x_tok[:, t, cols], in0=bank[2 * t + hf][:, :],
                                                         scalar=moments[:, t, 0:1], in1=ln_rows[:, 0, cols],
                                                         op0=ALU.subtract, op1=ALU.mult))
                dve.wait_ge(final_std, t + 1)
                final(nc.vector.reciprocal(rstd[:, t:t + 1], std[:, t:t + 1]))
                for hf in range(2):
                    cols = slice(hf * HALF, (hf + 1) * HALF)
                    nc.vector.scalar_tensor_tensor(out=x_tok[:, t, cols], in0=x_tok[:, t, cols],
                                                   scalar=rstd[:, t:t + 1], in1=ln_rows[:, 1, cols],
                                                   op0=ALU.mult, op1=ALU.add).then_inc(out_ready, 1)

        @block.gpsimd
        def _(pool):
            count = [0]

            def step(ins):
                count[0] += 1
                ins.then_inc(pool_chain, 1)
                pool.wait_ge(pool_chain, count[0])

            nc.gpsimd.memset(b_ada_raw, 0.0).then_inc(raw_cleared, 1)
            pool.wait_ge(job_read, JOB_GATES)
            src = xp_t
            for k in range(PG):
                dst = (mixed, pool_tmp)[k % 2]
                if k == 1:
                    pool.wait_ge(ld_bias, 96)
                step(nc.gpsimd.tensor_copy(dst[:, k:PG, 0:1 << k], src[:, k:PG, 0:1 << k]))
                step(nc.gpsimd.tensor_tensor(dst[:, k:PG, 1 << k:S], src[:, k:PG, 1 << k:S],
                                             src[:, k:PG, 0:S - (1 << k)], ALU.add))
                src = dst
            for g, w in enumerate(POOL_WINDOWS):
                sums = (mixed, pool_tmp)[g % 2]
                rcnt = const[:, C_RCNT + 16 * g:C_RCNT + 16 * g + 16]
                step(nc.gpsimd.tensor_tensor(mixed[:, g, 0:16], sums[:, g, 0:16], rcnt, ALU.mult))
                step(nc.gpsimd.tensor_scalar(mixed[:, g, 16:S], sums[:, g, 16:S], 1.0 / w, None, ALU.mult))
            nc.gpsimd.tensor_tensor(mixed, mixed, xp_t, ALU.subtract).then_inc(pooled, 1)

            pool.wait_ge(merged, KT // 2)
            nc.gpsimd.memset(y, 0.0).then_inc(y_cleared, 1)
            pool.wait_ge(moments_ready, 2 + 2 * NT - 1)
            nc.gpsimd.memset(scatter, 0.0).then_inc(moe_cleared, 1)
            for t, m, parts in ((0, 0, 1), (0, 1, 2), (1, 1, 4)):
                pool.wait_ge(part_ready, parts)
                pool.wait_ge(u2_t_done, 2 * (t + 1))
                nc.gpsimd.tensor_tensor(u2[:, t, :], u2[:, t, :], u2_parts[:, m, t, :], ALU.subtract) \
                  .then_inc(rest_ready, 1)
            pool.wait_ge(part_ready, 3 * NT)
            nc.gpsimd.memset(scatter_t[:, 1], 0.0).then_inc(scatter_t_cleared, 1)
            pool.wait_ge(ld_b_down, 32)
            pool.wait_ge(gate2_ready, 1)
            pool.wait_ge(weight_t_ready, 1)
            nc.gpsimd.tensor_tensor(y, y, gate2_halves, ALU.mult).then_inc(y_ready, 1)
            pool.wait_ge(most_f_ready, 1)
            nc.gpsimd.partition_all_reduce(most_all, most_f, P, bass.bass_isa.ReduceOp.max).then_inc(most_all_ready, 1)
            pool.wait_ge(most_all_ready, 1)
            nc.gpsimd.tensor_copy(most_i, most_all).then_inc(most_ready, 1)

        @block.tensor
        def _(pe):
            pe.wait_ge(ld_const, 16)
            for t in range(NT):
                pe.wait_ge(xn_ready, t + 1)
                for k in range(KT):
                    last = nc.tensor.transpose(bank[k // 2][:, (k % 2) * S + t * P:(k % 2) * S + (t + 1) * P],
                                               xn[:, t, k * P:(k + 1) * P], ident)
            last.then_inc(xn_t_done, 1)

            pe.wait_ge(silu_ready, 1)
            for j in range(4):
                landed(pe, ("ada", j))
                w = unit_view(("ada", j))
                for q in range(4):
                    for k in range(DVE_KT, KT):
                        nc.tensor.matmul(bank[4 + q][:, j:j + 1], w[:, k, q * P:(q + 1) * P], c_silu[:, k:k + 1],
                                         start=k == DVE_KT, stop=False)
                if j == 0:
                    pe.wait_ge(pick_ready, 1)
                    pe.wait_ge(parts_ready, 1)
                for q in range(4):
                    nc.tensor.matmul(bank[4 + q][:, j:j + 1], ada_parts[:, q * P:(q + 1) * P],
                                     pick_rows[0:96, j:j + 1], start=False, stop=False)
                pe.wait_ge(acc_ready, j + 1)
                for q in range(4):
                    last = nc.tensor.matmul(bank[4 + q][:, j:j + 1], ada_acc[:, j % 2, q * P:(q + 1) * P], one,
                                            start=False, stop=True)
                last.then_inc(acc_read, 1)

            def row(j, dst=bank[5]):
                pe.wait_ge(acc_ready, j + 1)
                if 4 < j < 10:
                    pe.wait_ge(row_ready, j - 4)
                nc.tensor.matmul(dst[:, :], one.to_broadcast([P, P]), ada_acc[:, j % 2, :],
                                 start=True, stop=False)
                nc.tensor.matmul(dst[:, :], pick_rows[0:96, j:j + 1].to_broadcast([96, P]), ada_parts[:, :],
                                 start=False, stop=True).then_inc(acc_read, 1)

            def job(n):
                u, part = jobs[n]
                w, dst = unit_view(u), job_bank(n)
                if n >= 2:
                    pe.wait_ge(job_read, n - 1)
                landed(pe, u)
                if u[1] in (4, 5):
                    for t in ((part,) if u[1] == 4 else range(NT)):
                        cols = slice(0, HALF) if u[1] == 4 else slice(t * S, (t + 1) * S)
                        for k in range(KT):
                            last = nc.tensor.matmul(dst[:, cols], u_t[:, k, t * P:(t + 1) * P], w[:, k, :],
                                                    start=k == 0, stop=k == KT - 1)
                else:
                    for q in range(2):
                        f = 2 * part + q
                        for k in range(KT):
                            if n == 0 and q == 0:
                                pe.wait_ge(u_t_ready, k + 1)
                            last = nc.tensor.matmul(dst[:, q * S:(q + 1) * S], w[:, k, f * P:(f + 1) * P],
                                                    u_t[:, k, :], start=k == 0, stop=k == KT - 1)
                last.then_inc(job_done, 1)

            def partner(n):
                pe.wait_ge(job_read, n + 1)
                if n >= 2:
                    pe.wait_ge(rotated, n - 1)
                nc.tensor.matmul(bank[2 + n % 2][:, :], const[:, C_PERM:C_PERM + P],
                                 qk[:, 2 * n:2 * n + 2, :].rearrange("p j t -> p (j t)"),
                                 start=True, stop=True).then_inc(partner_done, 1)

            job(0)
            for n in range(1, 7):
                job(n)
                partner(n - 1)
            row(4)
            job(7)
            job(8)
            row(5)
            job(9)
            job(10)
            row(6)

            pe.wait_ge(rotated, QT)
            for s in range(HEAD_SLOTS):
                for t in range(NT):
                    for g in range(NG):
                        head = g * HEAD_SLOTS + s
                        rows = slice(HEAD_DIM * (head % 2), HEAD_DIM * (head % 2 + 1))
                        q = qk[rows, head // 2, t * P:(t + 1) * P]
                        keys = qk[rows, QT + head // 2, 0:(t + 1) * P]
                        dst = bank[0][:, g * P:(g + 1) * P] if t == 0 else \
                            bank[1 + g // 2][:, (g % 2) * S:(g % 2 + 1) * S]
                        last = nc.tensor.matmul(dst, q, keys, start=True, stop=True)
                    last.then_inc(scores_done, 1)
                job(JOB_GATES + 2 * s)
                pe.wait_ge(probs_ready, 2 * (s + 1))
                for g in range(NG):
                    dst = bank[T_BANKS[g]]
                    nc.tensor.transpose(dst[:, 0:P], probs[:, g * P:(g + 1) * P], ident)
                    for k in range(NT):
                        last = nc.tensor.transpose(dst[:, (k + 1) * P:(k + 2) * P],
                                                   probs[:, 384 + g * S + k * P:384 + g * S + (k + 1) * P], ident)
                    last.then_inc(probs_t_done, 1)
                rows = slice(HEAD_DIM * (s % 2), HEAD_DIM * (s % 2 + 1))
                for g in range(NG):
                    pe.wait_ge(probs_t_read, NG * s + g + 1)
                    cols = slice((g * HEAD_SLOTS + s) * HEAD_DIM, (g * HEAD_SLOTS + s + 1) * HEAD_DIM)
                    c0 = (s // 2) * S
                    nc.tensor.matmul(bank[3][rows, c0:c0 + S], v_tok[:, 0, cols], probs_t[:, g, 0:S],
                                     start=g == 0, stop=False)
                    last = nc.tensor.matmul(bank[3][rows, c0 + P:c0 + S], v_tok[:, 1, cols], probs_t[:, g, S:S + P],
                                            start=False, stop=g == NG - 1)
                if s == HEAD_SLOTS - 1:
                    last.then_inc(attn_done, 1)
                if s >= 1:
                    row(6 + s)
                job(JOB_GATES + 2 * s + 1)

            pe.wait_ge(ld_pool, 32)
            pe.wait_ge(pooled, 1)
            for n in range(2):
                pe.wait_ge(job_read, JOB_POOL + n - 1)
                for q in range(2):
                    g = 2 * n + q
                    last = nc.tensor.matmul(job_bank(JOB_POOL + n)[:, q * S:(q + 1) * S], pool_w_sb[:, g, :],
                                            mixed[:, g, :], start=True, stop=True)
                last.then_inc(job_done, 1)

            pe.wait_ge(job_read, JOB_POOL + 2)
            pe.wait_ge(attn_t_ready, 1)
            wp, wa = unit_view(("pool_out", 0)), unit_view(("attn_out", 0))
            landed(pe, ("attn_out", 0))
            landed(pe, ("pool_out", 0))
            for n in range(KT // 2):
                if n >= 2:
                    pe.wait_ge(merged, n - 1)
                for w, src, kk, b in ((wp, xp_t, 4, 6), (wa, attn_t, 2, 0)):
                    for q in range(2):
                        f = 2 * n + q
                        for k in range(kk):
                            last = nc.tensor.matmul(bank[b + n % 2][:, q * S:(q + 1) * S],
                                                    w[:, k, f * P:(f + 1) * P], src[:, k, :],
                                                    start=k == 0, stop=k == kk - 1)
                last.then_inc(branch_done, 1)

            pe.wait_ge(row_ready, 6)
            for t in range(NT):
                for hf in range(2):
                    for k in range(KT):
                        u = ("o", k // 4)
                        if t == 0 and hf == 0 and k % 4 == 0:
                            landed(pe, u)
                        if t == 0 and hf == 0 and k % 2 == 0:
                            pe.wait_ge(merged, k // 2 + 1)
                        last = nc.tensor.matmul(bank[2 + 2 * t + hf][:, :], gates[:, k, t * P:(t + 1) * P],
                                                unit_view(u)[:, k % 4, hf * HALF:(hf + 1) * HALF],
                                                start=k == 0, stop=k == KT - 1)
                    last.then_inc(mix_done, 1)

            for t in range(NT):
                for k in range(KT):
                    if k % 4 == 0:
                        pe.wait_ge(u2_ready, 2 * t + k // 4 + 1)
                    last = nc.tensor.transpose(bank[6 + k // 4][:, (k % 4) * P:(k % 4 + 1) * P],
                                               u2[:, t, k * P:(k + 1) * P], ident)
                    if k % 4 == 3:
                        last.then_inc(u2_t_done, 1)
                if t == 0:
                    pe.wait_ge(moments_ready, 3)
                    row(10, bank[2])
                    row(11, bank[3])
                    pe.wait_ge(ld_router, 32)
                for k in range(KT):
                    if k % 4 == 0:
                        pe.wait_ge(u2_t_ready, 2 * t + k // 4 + 1)
                    nc.tensor.matmul(bank[4 + t][:, 0:NE], u_t[:, k, t * P:(t + 1) * P], router_w[:, k, :],
                                     start=k == 0, stop=False)
                nc.tensor.matmul(bank[4 + t][:, 0:NE], one[0:1, :].to_broadcast([1, P]), b_router_sb,
                                 start=False, stop=True).then_inc(logits_done, 1)
                for n in ((0, 1, 2), (3,))[t]:
                    if n == 0:
                        pe.wait_ge(scaled_ready, 1)
                    if n == 2:
                        pe.wait_ge(moments_ready, 2 + 2 * NT)
                        pe.wait_ge(row_ready, 8)
                    nc.tensor.matmul(bank[n][:, :], scaled_ident, x_tok[:, n // 2, (n % 2) * HALF:(n % 2 + 1) * HALF],
                                     start=True, stop=False).then_inc(seeded, 1)

            pe.wait_ge(weight_ready, 1)
            pe.wait_ge(tri_ready, 1)
            nc.tensor.matmul(Y_BANK[:, 0:NE], tri_bf, chosen[:, 0, :], start=True, stop=True)
            nc.tensor.matmul(Y_BANK[:, NE:2 * NE], one_bf[:, 0:1].to_broadcast([P, P]), chosen[:, 0, :],
                             start=True, stop=False)
            nc.tensor.matmul(Y_BANK[:, NE:2 * NE], tri_bf, chosen[:, 1, :], start=False, stop=True) \
              .then_inc(rank_done, 1)
            for t in range(NT):
                for hf in range(2):
                    last = nc.tensor.matmul(U_BANK[hf * CAP:hf * CAP + NE, t * P:(t + 1) * P],
                                            weight[:, t, 0:NE], ident, start=True, stop=True)
            last.then_inc(weight_t_done, 1)

            def gather(b):
                for k in range(KT):
                    for t in range(NT):
                        for m in range(3):
                            last = nc.tensor.matmul(M_BANK[:, k * CAP:(k + 1) * CAP],
                                                    u2_parts[:, m, t, k * P:(k + 1) * P], pick_tok[:, b, t, :],
                                                    start=(t, m) == (0, 0), stop=(t, m) == (NT - 1, 2))
                return last

            def transpose_scatter():
                for t in range(NT):
                    for hf in range(2):
                        start = 64 - 64 * hf
                        n = 2 * t + hf
                        last = nc.tensor.transpose(M_BANK[:, n * P:(n + 1) * P], scatter[:, t, start:start + P],
                                                   ident)
                return last

            def stream(dst, lhs, tiles, k0, first, last_one):
                for k in range(4):
                    for hf in range(2):
                        last = nc.tensor.matmul(dst[hf * CAP:(hf + 1) * CAP, :], lhs(k0 + k),
                                                tiles[k][:, hf * HALF:(hf + 1) * HALF],
                                                start=first and k == 0, stop=last_one and k == 3)
                return last

            def add_bias(dst, b, which):
                for hf in range(2):
                    last = nc.tensor.matmul(dst[hf * CAP:(hf + 1) * CAP, :], pick_bias[:, b, :],
                                            bias_parts[:, which, hf * HALF:(hf + 1) * HALF],
                                            start=False, stop=True)
                return last

            def ring_tiles(m):
                return [expert_view(m)[:, k, :] for k in range(4)]

            def hidden_t(kt):
                return h_t[:, kt % 4, (kt // 4) * CAP:(kt // 4 + 1) * CAP]

            def transpose_hidden():
                for k in range(4):
                    last = nc.tensor.transpose(M_BANK[:, k * P:(k + 1) * P], h[:, k * P:(k + 1) * P], ident)
                return last

            def combine(t, b, values, stop, done=None):
                for hf in range(2):
                    last = nc.tensor.matmul(bank[2 * t + hf][:, :], scatter_t[:, b, 2 * t + hf, :], values,
                                            start=False, stop=stop)
                    if done is not None:
                        last.then_inc(done, 1)
                return last

            pe.wait_ge(picked, 1)
            pe.wait_ge(part_ready, 3 * NT)
            gather(0).then_inc(gather_done, 1)

            def turn(i, first):
                for j in range(BODY):
                    n0 = UNITS * j
                    b = j % 2

                    def unit_landed(k):
                        n = n0 + k
                        if first and SLOTS <= n < SLOTS + EXTRA:
                            pe.wait_ge(extra_landed[n - SLOTS], 32)
                            return
                        m = n if first and n < SLOTS else n - EXTRA
                        s = RING[m % SLOTS]
                        pe.wait_ge(slot_landed[s], i * (16 * BODY * UNITS // SLOTS) + 16 * (FILLS[s] + m // SLOTS + 1))

                    def tiles(k):
                        n = n0 + k
                        if first and SLOTS <= n < SLOTS + EXTRA:
                            return extra_tiles[n - SLOTS]
                        return ring_tiles(n if first and n < SLOTS else n - EXTRA)

                    for k in range(2):
                        unit_landed(k)
                        if k == 0:
                            pe.wait_ge(misc_read, i * (3 * BODY) + (3 * j + 1))
                        stream(G_BANK, lambda kt: x_sel[:, b, kt, :], tiles(k), 4 * k, k == 0, False) \
                            .then_inc(pe_unit_used, 1)
                        if k == 0:
                            pe.wait_ge(picked, i * BODY + (j + 2))
                            gather(1 - b).then_inc(gather_done, 1)
                    add_bias(G_BANK, b, 0).then_inc(gate_done, 1)
                    pe.wait_ge(scatter_ready, i * BODY + (j + 1))
                    pe.wait_ge(misc_read, i * (3 * BODY) + (3 * j + 2))
                    transpose_scatter().then_inc(scatter_t_done, 1)
                    for k in range(2):
                        unit_landed(2 + k)
                        stream(U_BANK, lambda kt: x_sel[:, b, kt, :], tiles(2 + k), 4 * k, k == 0, False) \
                            .then_inc(pe_unit_used, 1)
                        if k == 0:
                            pe.wait_ge(y_ready, i * BODY + (j + 1))
                            combine(0, 1 - b, y, False)
                    add_bias(U_BANK, b, 1).then_inc(up_done, 1)
                    combine(1, 1 - b, y, False)
                    pe.wait_ge(h_ready, i * BODY + (j + 1))
                    pe.wait_ge(misc_read, i * (3 * BODY) + (3 * j + 3))
                    transpose_hidden().then_inc(h_t_done, 1)
                    pe.wait_ge(misc_read, i * (3 * BODY) + (3 * j + 4))
                    for k in range(2):
                        unit_landed(4 + k)
                        stream(Y_BANK, hidden_t, tiles(4 + k), 4 * k, k == 0, k == 1) \
                            .then_inc(pe_unit_used, 1)
            turn(0, True)
            with pe.Fori(1, TURNS) as i:
                turn(i, False)

            pe.wait_ge(most_ready, 1)
            most = pe.value_load(most_i[0:1, :], min_val=0, max_val=S)
            with pe.If(most > CAP):
                pe.wait_ge(y_ready, NE + 1)
                pe.sem_inc(ovf_pe, 1)
                with pe.Fori(0, NE) as e:
                    pe.wait_ge(ovf_landed, e * (16 * UNITS) + 16 * UNITS)
                    for n in range(CHUNKS):
                        def act_step(k):
                            pe.wait_ge(ovf_act, e * (4 * CHUNKS) + (4 * n + k))

                        def dve_step(k):
                            pe.wait_ge(ovf_dve, e * (4 * CHUNKS) + (4 * n + k))

                        dve_step(1)
                        gather(0).then_inc(ovf_pe, 1)
                        act_step(1)
                        transpose_scatter().then_inc(ovf_pe, 1)
                        act_step(2)
                        for k in range(2):
                            stream(G_BANK, lambda kt: x_sel[:, 0, kt, :], ring_tiles(k), 4 * k, k == 0, False)
                        add_bias(G_BANK, 0, 0)
                        for k in range(2):
                            stream(U_BANK, lambda kt: x_sel[:, 0, kt, :], ring_tiles(2 + k), 4 * k, k == 0, False)
                        add_bias(U_BANK, 0, 1).then_inc(ovf_pe, 1)
                        dve_step(3)
                        transpose_hidden().then_inc(ovf_pe, 1)
                        act_step(4)
                        for k in range(2):
                            last = stream(Y_BANK, hidden_t, ring_tiles(4 + k), 4 * k, k == 0, k == 1)
                        last.then_inc(ovf_pe, 1)
                        dve_step(4)
                        for t in range(NT):
                            last = combine(t, 0, y_late, False)
                        last.then_inc(ovf_pe, 1)

            pe.wait_ge(y_ready, NE + 1)
            for t in range(NT):
                combine(t, (NE - 1) % 2, y, True, combined)


INPUTS = ["x", "c", "positions", "w_ada", "b_ada", "w_in", "pool_w", "pool_scale", "w_pool_out", "w_attn_out",
          "w_o", "ln1_g", "ln1_b", "w_router", "b_router", "w_gate", "b_gate", "w_up", "b_up", "w_down", "b_down",
          "ln2_g", "ln2_b"]


def kernel(**inputs):
    import concourse.bacc as bacc
    from concourse.bass_utils import run_bass_kernel_spmd

    nc = bacc.Bacc("TRN2", target_bir_lowering=False, num_devices=1)
    const_table, mask_table = constants()
    arrays = {name: np.ascontiguousarray(inputs[name]) for name in INPUTS}
    arrays["const_table"], arrays["mask_table"] = const_table, mask_table
    aps = [nc.dram_tensor(name, a.shape, mybir.dt.from_np(a.dtype), kind="ExternalInput").ap()
           for name, a in arrays.items()]
    out = nc.dram_tensor("out", (1, S, D), F32, kind="ExternalOutput").ap()
    layer_kernel(nc, *aps, out)
    r = run_bass_kernel_spmd(nc, [arrays], core_ids=[0])
    return r.results[0]["out"]
```
